# Optimizing a Trainium2 kernel written in Bass

```python
import jax, jax.numpy as jnp
from jax import lax
import numpy as np

D_MODEL = 1024
BATCH = 1
SEQ = 256
DEPTH = 2

MIX_W = 512
N_BRANCH = 4
POOL_WINDOWS = (2, 4, 8, 16)
POOL_GROUPS = 4
POOL_GW = MIX_W // POOL_GROUPS
ATT_HEADS = 8
ATT_KV_HEADS = 2
HEAD_DIM = 64
ROPE_DIM = HEAD_DIM // 4
ROPE_THETA = 500000.0
IDX_HEADS = 8
IDX_DIM = 32
IDX_ROPE_DIM = IDX_DIM // 4
TOPK_MAX = 256
Q_BLOCK = 128
CONV_KERNEL = 31
SSM_HEADS = 8
SSM_HEAD_DIM = 64
SSM_GROUPS = 2
SSM_STATE = 64
SSM_CONV = 4
SSM_XBC = MIX_W + 2 * SSM_GROUPS * SSM_STATE
SSM_CHUNK = 128
D_FF = 2816
N_EXPERTS = 8
TOP_K = 2
D_FF_EXPERT = 3584
N_DENSE = (DEPTH + 1) // 2
N_MOE = DEPTH // 2
NORM_EPS = 1e-6
SPLIT_SIZES = (MIX_W, ATT_HEADS * HEAD_DIM, 2 * ATT_KV_HEADS * HEAD_DIM, IDX_HEADS * IDX_DIM, IDX_DIM, IDX_HEADS,
               2 * MIX_W, MIX_W, SSM_XBC, SSM_HEADS, N_BRANCH * D_MODEL)
IN_W = sum(SPLIT_SIZES)

kernel_name = 'hybrid_pool_dsa_conformer_ssd_moe'

def rms_norm(x, g):
    xf = x.astype(jnp.float32)
    y = xf * lax.rsqrt(jnp.mean(xf * xf, axis=-1, keepdims=True) + NORM_EPS)
    return (y * g.astype(jnp.float32)).astype(x.dtype)

def layer_norm(x, g, b):
    xf = x.astype(jnp.float32)
    mu = jnp.mean(xf, axis=-1, keepdims=True)
    xc = xf - mu
    y = xc * lax.rsqrt(jnp.mean(xc * xc, axis=-1, keepdims=True) + NORM_EPS)
    return (y * g.astype(jnp.float32) + b.astype(jnp.float32)).astype(x.dtype)

def rope_partial(x, rot_dim):
    seq = x.shape[1]
    half = rot_dim // 2
    inv_freq = jnp.power(jnp.float32(ROPE_THETA), -jnp.arange(half, dtype=jnp.float32) * (2.0 / rot_dim))
    ang = jnp.arange(seq, dtype=jnp.float32)[:, None] * inv_freq[None, :]
    cos = jnp.cos(ang)[None, :, None, :]
    sin = jnp.sin(ang)[None, :, None, :]
    xf = x.astype(jnp.float32)
    x1 = xf[..., :half]
    x2 = xf[..., half:rot_dim]
    out = jnp.concatenate([x1 * cos - x2 * sin, x2 * cos + x1 * sin, xf[..., rot_dim:]], axis=-1)
    return out.astype(x.dtype)

def causal_depthwise_conv(x, w, b):
    width, ch = w.shape
    y = lax.conv_general_dilated(x, w[:, None, :].astype(x.dtype), window_strides=(1,),
                                 padding=[(width - 1, 0)], dimension_numbers=('NWC', 'WIO', 'NWC'),
                                 feature_group_count=ch)
    return y + b.astype(x.dtype)

def pool_mixer(u, w_grp, scale):
    bsz, seq, _ = u.shape
    uf = u.astype(jnp.float32)
    csum = jnp.cumsum(uf, axis=1)
    t = jnp.arange(seq)
    means = []
    for g, win in enumerate(POOL_WINDOWS):
        cs = csum[..., g * POOL_GW:(g + 1) * POOL_GW]
        cs_prev = jnp.pad(cs, ((0, 0), (win, 0), (0, 0)))[:, :seq]
        cnt = jnp.minimum(t + 1, win).astype(jnp.float32)[None, :, None]
        means.append((cs - cs_prev) / cnt)
    p = (jnp.concatenate(means, axis=-1) - uf).reshape(bsz, seq, POOL_GROUPS, POOL_GW)
    y = jnp.einsum('bsgc,gcd->bsgd', p, w_grp.astype(jnp.float32)).reshape(bsz, seq, MIX_W)
    return (y * scale.astype(jnp.float32)).astype(u.dtype)

def dsa_attention(q, k, v, q_idx, k_idx, w_idx):
    bsz, seq, n_heads, hd = q.shape
    n_kv = k.shape[2]
    top_k = min(TOPK_MAX, seq // 4)
    n_blocks = seq // Q_BLOCK
    key_pos = jnp.arange(seq)
    scale = hd ** -0.5
    gather = jax.vmap(lambda a, i: a[i])

    def to_blocks(a):
        return jnp.moveaxis(a.reshape((bsz, n_blocks, Q_BLOCK) + a.shape[2:]), 1, 0)

    def one_block(args):
        qb, qib, wb, t0 = args
        pos_q = t0 + jnp.arange(Q_BLOCK)
        s_h = jax.nn.relu(jnp.einsum('bqhd,bsd->bqhs', qib, k_idx))
        score = jnp.einsum('bqhs,bqh->bqs', s_h, wb).astype(jnp.float32)
        causal = key_pos[None, :] <= pos_q[:, None]
        score = jnp.where(causal[None], score, -jnp.inf)
        _, idx = lax.top_k(score, top_k)
        valid = idx <= pos_q[None, :, None]
        ks = gather(k, idx)
        vs = gather(v, idx)
        qg = qb.reshape(bsz, Q_BLOCK, n_kv, n_heads // n_kv, hd)
        logits = jnp.einsum('bqgrd,bqkgd->bqgrk', qg, ks).astype(jnp.float32) * scale
        logits = jnp.where(valid[:, :, None, None, :], logits, -jnp.inf)
        p = jax.nn.softmax(logits, axis=-1).astype(v.dtype)
        o = jnp.einsum('bqgrk,bqkgd->bqgrd', p, vs)
        return o.reshape(bsz, Q_BLOCK, n_heads * hd)

    out = lax.map(one_block, (to_blocks(q), to_blocks(q_idx), to_blocks(w_idx),
                              jnp.arange(n_blocks) * Q_BLOCK))
    return jnp.moveaxis(out, 0, 1).reshape(bsz, seq, n_heads * hd)

def conformer_conv(u, dw, db, ln_g, ln_b):
    a, gt = jnp.split(u, 2, axis=-1)
    y = a * jax.nn.sigmoid(gt)
    y = causal_depthwise_conv(y, dw, db)
    return jax.nn.silu(layer_norm(y, ln_g, ln_b))

def ssd_scan(x, dt, a, bm, cm):
    bsz, seq, nh, hp = x.shape
    ng, ns = bm.shape[2], bm.shape[3]
    rep = nh // ng
    nc = seq // SSM_CHUNK
    xd = (x.astype(jnp.float32) * dt[..., None]).reshape(bsz, nc, SSM_CHUNK, nh, hp)
    da = (dt * a).reshape(bsz, nc, SSM_CHUNK, nh).transpose(0, 3, 1, 2)
    bc = bm.astype(jnp.float32).reshape(bsz, nc, SSM_CHUNK, ng, ns)
    cc = cm.astype(jnp.float32).reshape(bsz, nc, SSM_CHUNK, ng, ns)
    a_cum = jnp.cumsum(da, axis=-1)
    tri = jnp.tril(jnp.ones((SSM_CHUNK, SSM_CHUNK), dtype=bool))
    seg = a_cum[..., :, None] - a_cum[..., None, :]
    lmat = jnp.exp(jnp.where(tri, seg, -jnp.inf)).transpose(0, 2, 1, 3, 4)
    cb = jnp.repeat(jnp.einsum('bclgn,bcsgn->bcgls', cc, bc), rep, axis=2)
    y_diag = jnp.einsum('bchls,bcshp->bclhp', cb * lmat, xd)
    bh = jnp.repeat(bc, rep, axis=3)
    ch = jnp.repeat(cc, rep, axis=3)
    decay_states = jnp.exp(a_cum[..., -1:] - a_cum)
    states = jnp.einsum('bclhn,bhcl,bclhp->bchpn', bh, decay_states, xd)
    chunk_decay = jnp.moveaxis(jnp.exp(a_cum[..., -1]), 2, 0)

    def step(carry, inp):
        dec, st = inp
        return carry * dec[..., None, None] + st, carry

    init = jnp.zeros((bsz, nh, hp, ns), jnp.float32)
    _, prev = lax.scan(step, init, (chunk_decay, jnp.moveaxis(states, 1, 0)))
    prev = jnp.moveaxis(prev, 0, 1)
    y_off = jnp.einsum('bclhn,bchpn,bhcl->bclhp', ch, prev, jnp.exp(a_cum))
    return (y_diag + y_off).reshape(bsz, seq, nh, hp)

def mamba2_mixer(z, xbc, dt_raw, conv_w, conv_b, dt_bias, a_log, d_skip, norm_g):
    bsz, seq, _ = xbc.shape
    xbc = jax.nn.silu(causal_depthwise_conv(xbc, conv_w, conv_b))
    xs, bm, cm = jnp.split(xbc, [MIX_W, MIX_W + SSM_GROUPS * SSM_STATE], axis=-1)
    xs = xs.reshape(bsz, seq, SSM_HEADS, SSM_HEAD_DIM)
    bm = bm.reshape(bsz, seq, SSM_GROUPS, SSM_STATE)
    cm = cm.reshape(bsz, seq, SSM_GROUPS, SSM_STATE)
    dt = jax.nn.softplus(dt_raw.astype(jnp.float32) + dt_bias.astype(jnp.float32))
    a = -jnp.exp(a_log.astype(jnp.float32))
    y = ssd_scan(xs, dt, a, bm, cm) + d_skip.astype(jnp.float32)[:, None] * xs.astype(jnp.float32)
    y = y.reshape(bsz, seq, MIX_W) * jax.nn.silu(z.astype(jnp.float32))
    return rms_norm(y, norm_g)

def hybrid_mixer(h, w_in, pool_w, pool_scale, conv_dw, conv_b, conv_ln_g, conv_ln_b,
                 ssm_conv_w, ssm_conv_b, ssm_dt_bias, ssm_a_log, ssm_d, ssm_norm, w_br, w_out):
    bsz, seq, _ = h.shape
    offsets = np.cumsum(SPLIT_SIZES)[:-1].tolist()
    (u_pool, q, kv, qi, ki, wi, u_conv, z, xbc, dt_raw, gate_logits) = jnp.split(h @ w_in, offsets, axis=-1)
    y_a = pool_mixer(u_pool, pool_w, pool_scale)
    q = rope_partial(q.reshape(bsz, seq, ATT_HEADS, HEAD_DIM), ROPE_DIM)
    k, v = jnp.split(kv, 2, axis=-1)
    k = rope_partial(k.reshape(bsz, seq, ATT_KV_HEADS, HEAD_DIM), ROPE_DIM)
    v = v.reshape(bsz, seq, ATT_KV_HEADS, HEAD_DIM)
    qi = rope_partial(qi.reshape(bsz, seq, IDX_HEADS, IDX_DIM), IDX_ROPE_DIM)
    ki = rope_partial(ki.reshape(bsz, seq, 1, IDX_DIM), IDX_ROPE_DIM)[:, :, 0, :]
    y_b = dsa_attention(q, k, v, qi, ki, wi)
    y_c = conformer_conv(u_conv, conv_dw, conv_b, conv_ln_g, conv_ln_b)
    y_d = mamba2_mixer(z, xbc, dt_raw, ssm_conv_w, ssm_conv_b, ssm_dt_bias, ssm_a_log, ssm_d, ssm_norm)
    branches = jnp.stack([y_a.astype(h.dtype), y_b.astype(h.dtype), y_c.astype(h.dtype), y_d.astype(h.dtype)], axis=2)
    u = jnp.einsum('bsnc,ncd->bsnd', branches, w_br)
    gates = jax.nn.sigmoid(gate_logits.reshape(bsz, seq, N_BRANCH, D_MODEL))
    merged = jnp.einsum('bsnd,bsnd->bsd', gates, u)
    return merged @ w_out

def swiglu(h, wg, wu, wd):
    return (jax.nn.silu(h @ wg) * (h @ wu)) @ wd

def moe_swiglu(h, router, wg, wu, wd):
    logits = (h @ router).astype(jnp.float32)
    top_val, top_idx = lax.top_k(logits, TOP_K)
    probs = jax.nn.softmax(top_val, axis=-1)
    combine = jnp.einsum('bske,bsk->bse', jax.nn.one_hot(top_idx, N_EXPERTS, dtype=jnp.float32), probs)
    out = jnp.zeros(h.shape, jnp.float32)
    for e in range(N_EXPERTS):
        out = out + combine[..., e:e + 1] * swiglu(h, wg[e], wu[e], wd[e]).astype(jnp.float32)
    return out.astype(h.dtype)

def setup_inputs(seed: int = 0) -> dict:
    key = jax.random.key(seed)
    ks = iter(jax.random.split(key, 32))
    f32 = jnp.float32

    def nrm(shape, s):
        return jax.random.normal(next(ks), shape, f32) * s

    L, D = DEPTH, D_MODEL
    x = nrm((BATCH, SEQ, D), 1.0)
    norm_mix = 1.0 + nrm((L, D), 0.02)
    w_in = nrm((L, D, IN_W), D ** -0.5)
    pool_w = nrm((L, POOL_GROUPS, POOL_GW, POOL_GW), POOL_GW ** -0.5)
    pool_scale = 1.0 + nrm((L, MIX_W), 0.1)
    conv_dw = nrm((L, CONV_KERNEL, MIX_W), CONV_KERNEL ** -0.5)
    conv_b = nrm((L, MIX_W), 0.02)
    conv_ln_g = 1.0 + nrm((L, MIX_W), 0.02)
    conv_ln_b = nrm((L, MIX_W), 0.02)
    ssm_conv_w = nrm((L, SSM_CONV, SSM_XBC), SSM_CONV ** -0.5)
    ssm_conv_b = nrm((L, SSM_XBC), 0.02)
    dt0 = jnp.exp(jax.random.uniform(next(ks), (L, SSM_HEADS), f32, jnp.log(1e-3), jnp.log(1e-1)))
    ssm_dt_bias = dt0 + jnp.log(-jnp.expm1(-dt0))
    ssm_a_log = jnp.log(jax.random.uniform(next(ks), (L, SSM_HEADS), f32, 1.0, 16.0))
    ssm_d = 1.0 + nrm((L, SSM_HEADS), 0.1)
    ssm_norm = 1.0 + nrm((L, MIX_W), 0.02)
    w_br = nrm((L, N_BRANCH, MIX_W, D), MIX_W ** -0.5)
    w_out = nrm((L, D, D), D ** -0.5)
    norm_ffn = 1.0 + nrm((L, D), 0.02)
    ffn_w_gate = nrm((N_DENSE, D, D_FF), D ** -0.5)
    ffn_w_up = nrm((N_DENSE, D, D_FF), D ** -0.5)
    ffn_w_down = nrm((N_DENSE, D_FF, D), D_FF ** -0.5)
    moe_router = nrm((N_MOE, D, N_EXPERTS), D ** -0.5)
    moe_w_gate = nrm((N_MOE, N_EXPERTS, D, D_FF_EXPERT), D ** -0.5)
    moe_w_up = nrm((N_MOE, N_EXPERTS, D, D_FF_EXPERT), D ** -0.5)
    moe_w_down = nrm((N_MOE, N_EXPERTS, D_FF_EXPERT, D), D_FF_EXPERT ** -0.5)
    final_norm = 1.0 + nrm((D,), 0.02)
    return {'x': x, 'norm_mix': norm_mix, 'w_in': w_in, 'pool_w': pool_w, 'pool_scale': pool_scale,
            'conv_dw': conv_dw, 'conv_b': conv_b, 'conv_ln_g': conv_ln_g, 'conv_ln_b': conv_ln_b,
            'ssm_conv_w': ssm_conv_w, 'ssm_conv_b': ssm_conv_b, 'ssm_dt_bias': ssm_dt_bias,
            'ssm_a_log': ssm_a_log, 'ssm_d': ssm_d, 'ssm_norm': ssm_norm, 'w_br': w_br, 'w_out': w_out,
            'norm_ffn': norm_ffn, 'ffn_w_gate': ffn_w_gate, 'ffn_w_up': ffn_w_up, 'ffn_w_down': ffn_w_down,
            'moe_router': moe_router, 'moe_w_gate': moe_w_gate, 'moe_w_up': moe_w_up, 'moe_w_down': moe_w_down,
            'final_norm': final_norm}

def reference(x, norm_mix, w_in, pool_w, pool_scale, conv_dw, conv_b, conv_ln_g, conv_ln_b,
              ssm_conv_w, ssm_conv_b, ssm_dt_bias, ssm_a_log, ssm_d, ssm_norm, w_br, w_out,
              norm_ffn, ffn_w_gate, ffn_w_up, ffn_w_down, moe_router, moe_w_gate, moe_w_up, moe_w_down,
              final_norm):
    for layer in range(DEPTH):
        h = rms_norm(x, norm_mix[layer])
        x = x + hybrid_mixer(h, w_in[layer], pool_w[layer], pool_scale[layer], conv_dw[layer], conv_b[layer],
                             conv_ln_g[layer], conv_ln_b[layer], ssm_conv_w[layer], ssm_conv_b[layer],
                             ssm_dt_bias[layer], ssm_a_log[layer], ssm_d[layer], ssm_norm[layer],
                             w_br[layer], w_out[layer])
        h = rms_norm(x, norm_ffn[layer])
        j = layer // 2
        if layer % 2 == 0:
            x = x + swiglu(h, ffn_w_gate[j], ffn_w_up[j], ffn_w_down[j])
        else:
            x = x + moe_swiglu(h, moe_router[j], moe_w_gate[j], moe_w_up[j], moe_w_down[j])
    return rms_norm(x, final_norm)


_drawn_inputs = setup_inputs


def setup_inputs(seed=0):
    import zlib

    import numpy as np

    out = dict(_drawn_inputs(seed))
    spreads = {}
    factors = {}
    for name, (base, spread) in spreads.items():
        noise = np.random.default_rng([zlib.crc32(name.encode()), seed]).standard_normal(out[name].shape)
        drawn = base * np.exp(spread * noise) if base else spread * noise
        out[name] = __import__('jax').numpy.asarray(drawn.astype(out[name].dtype))
    for name, factor in factors.items():
        out[name] = (out[name] * factor).astype(out[name].dtype)
    return out
```

```python
import numpy as np
import concourse.bass as bass
from concourse import mybir
from contextlib import ExitStack

D = 1024
T = 256
NB = T // 128
KT = D // 128
MIX = 512
MG = MIX // 128
F_DENSE = 2816
F_EXP = 3584
NE = 8
CONV_W = 31
CPAD = CONV_W - 1
SSM_W = 4
SPAD = SSM_W - 1
PPAD = 16
TOPK = T // 4
HEADS = 8
EPS = 1e-6
FAR = -3.0e38
TAKEN = -3.4e38
SLAB = 512
PANEL = 4 * SLAB
STEP_F = 256
DENSE_STEPS = F_DENSE // STEP_F
EXP_STEPS = F_EXP // STEP_F
MIX_PANELS = 46
DENSE_PANELS = 3 * DENSE_STEPS
EXP_PANELS = 3 * EXP_STEPS
HRING = 3
MRING = 3
FRING = 6
EXTRA = 3
SLOTS = NE + EXTRA + 1

C_POOL, C_Q, C_KVQI, C_KIWI = 0, 512, 1024, 1536
C_A, C_GT, C_Z, C_XBC0, C_XBC1, C_GATE = 1576, 2088, 2600, 3112, 3624, 3888

CHUNKS = [("a", 2, "A"), ("gt", 2, "A"), ("kiwi", 2, "A"), ("kvqi", 2, "A"), ("q", 2, "A"), ("pool", 2, "A"),
          ("xbc0", 2, "A"), ("xbc1", 2, "A"), ("z", 2, "A"), ("g0h0", 2, "A"), ("g0h1", 2, "A"),
          ("pooly", 0, "A"), ("br0h0", 1, "D"), ("br0h1", 1, "D"),
          ("lnsum", 0, "D"), ("g2h0", 2, "A"), ("lnvar", 0, "D"), ("g2h1", 2, "A"),
          ("br2h0", 1, "D"), ("br2h1", 1, "D"), ("g1h0", 2, "A"), ("g1h1", 2, "A"),
          ("br1h0", 1, "D"), ("br1h1", 1, "D"), ("g3h0", 2, "A"), ("g3h1", 2, "A"),
          ("rmsum", 0, "D"), ("br3h0", 1, "D"), ("br3h1", 1, "D"), ("out0", 2, "D"), ("out1", 2, "D")]
BR_ORDER = [0, 2, 1, 3]
NCH = len(CHUNKS)
CH_INDEX = {c[0]: i for i, c in enumerate(CHUNKS)}
CH_PANEL = {}
_p = 0
for _n, _k, _e in CHUNKS:
    CH_PANEL[_n] = _p
    _p += _k
assert _p == MIX_PANELS
N_EVA = sum(1 for c in CHUNKS if c[2] == "A")
N_EVD = NCH - N_EVA

CONSTS = {}
_c = 0
for _n, _w in (("ident", 128), ("tri", 128), ("ones", 128), ("strict", 128), ("rotq", 128), ("roti", 128),
               ("swap", 128), ("cosq", 256), ("sinq", 256), ("cosi", 256), ("sini", 256), ("iota", 128),
               ("invcnt", 64), ("far", 256), ("causal", 128), ("rev8", 8), ("iota8", 8)):
    CONSTS[_n] = (_c, _w)
    _c += _w
NCONST = _c
PARAMS = {}
_c = 0
for _n, _w in (("pool_w", 512), ("pool_scale", 4), ("conv_dw", 4 * CONV_W), ("conv_b", 4), ("ln_g", 4), ("ln_b", 4),
               ("ssm_w", 24), ("ssm_b", 6), ("dskip", 4), ("ssm_norm", 4), ("dt_bias", 8), ("a_log", 8), ("router", 64)):
    PARAMS[_n] = (_c, _w)
    _c += _w
NPARAM = _c

A_P, A_YPAD, A_CACC, A_QK, A_IDX = 0, 2176, 3320, 4344, 5624
A_KI, A_V, A_UPAD, A_XBCP, A_XBC, A_Z, A_GATES = 6392, 6904, 7160, 8248, 9802, 11338, 12362
A_SCORE, A_MASK, A_MISC = 14410, 14794, 15178
A_END = 15178 + 400
A_RAW = 0
A_SG, A_HID = 3 * PANEL, 3 * PANEL + 1024


def build(nc, x_d, gains_d, consts_d, params_d, w_in, w_br, w_out, fg, fu, fd, mg, mu, md, out_d):
    f32, f32r, i32 = mybir.dt.float32, mybir.dt.float32r, mybir.dt.int32
    ALU, ACT, AX = mybir.AluOpType, mybir.ActivationFunctionType, mybir.AxisListType
    ctx = ExitStack()
    with ctx:
        def sb(name, shape, dt=f32):
            return ctx.enter_context(nc.sbuf_tensor(name, shape, dt))

        def sem(name):
            return ctx.enter_context(nc.semaphore(name))

        raw_ring = sb("raw_ring", [128, MRING * PANEL])
        hi_ring = sb("hi_ring", [128, HRING, PANEL], f32r)
        lo_ring = sb("lo_ring", [128, HRING, PANEL], f32r)
        x = sb("x", [128, NB, D])
        hT_hi = sb("hT_hi", [128, KT, T], f32r)
        hT_lo = sb("hT_lo", [128, KT, T], f32r)
        act_hi = sb("act_hi", [128, 2048], f32r)
        act_lo = sb("act_lo", [128, 2048], f32r)
        hid_hi = sb("hid_hi", [128, 2, STEP_F], f32r)
        hid_lo = sb("hid_lo", [128, 2, STEP_F], f32r)
        pick = sb("pick", [128, NB, 128], f32r)
        pickT = sb("pickT", [128, NB, 128], f32r)
        ident_r = sb("ident_r", [128, 128], f32r)
        rt_hi = sb("rt_hi", [128, 64], f32r)
        rt_lo = sb("rt_lo", [128, 64], f32r)
        consts = sb("consts", [128, NCONST])
        params = sb("params", [128, NPARAM])
        gain = sb("gain", [128, D])
        mrg = sb("mrg", [128, 2 * D])
        arena = sb("arena", [128, A_END])
        small = sb("small", [128, 64])
        meta = sb("meta", [1, 4], i32)
        pairs = [ctx.enter_context(nc.psum_tensor(f"pair{i}", [128, 1024], f32)) for i in range(2)]
        aux = ctx.enter_context(nc.psum_tensor("aux", [128, 2048], f32))

        def C(n):
            return consts[:, CONSTS[n][0]:CONSTS[n][0] + CONSTS[n][1]]

        def W(n, i=0, k=1):
            o = PARAMS[n][0]
            return params[:, o + i:o + i + k]

        def ar(o, n):
            return arena[:, o:o + n]

        def ar3(o, a, b):
            return arena[:, o:o + a * b].rearrange("p (a b) -> p a b", b=b)

        def raw(slot):
            if slot < MRING:
                return raw_ring[:, slot * PANEL:(slot + 1) * PANEL]
            return arena[:, A_RAW + (slot - MRING) * PANEL:A_RAW + (slot - MRING + 1) * PANEL]

        hN = mrg[:, :].rearrange("p (b d) -> p b d", b=NB)
        merged = mrg[:, :].rearrange("p (g t) -> p g t", t=T)

        raw_in = [sem(f"raw_in{i}") for i in range(FRING)]
        x_in, const_in, param_in, gain_in, stored = sem("x_in"), sem("const_in"), sem("param_in"), sem("gain_in"), sem("stored")
        hi_ready, lo_ready, panel_used = sem("hi_ready"), sem("lo_ready"), sem("panel_used")
        emptied = {"A": sem("emptied_by_act"), "D": sem("emptied_by_dve")}
        v_done, a_done = sem("v_done"), sem("a_done")
        names = ["squared", "meaned", "rooted", "normed", "turned", "hT_hi_done", "hT_lo_done",
                 "ki_turned", "ki_copied", "rotated", "roped", "k_swapped", "k_copied", "indexed", "relued", "scored",
                 "masked", "glued", "conved", "ln_summed", "centred", "ln_squared", "ln_varied", "ln_rooted",
                 "ln_scaled", "ln_sig", "pooled", "pool_mixed", "branch_f", "branch_hi", "branch_lo", "merged_done",
                 "merged_hi", "merged_lo", "logits_done", "logits_read", "negmax_done", "exped", "probs_done",
                 "probs_turned", "probs_copied", "attended", "att_copied", "xbc_sig", "xbc_done",
                 "dt_abs", "dt_exp", "dt_plus", "dt_ln", "dt_done", "a_exp", "xs_turned", "xd_done", "cb_done", "cbm_done",
                 "acol_done", "acol_read", "arow_done", "arow_read", "decay_exp", "mixm_done", "y_done", "y_read", "z_sig",
                 "gated", "rms_squared", "rms_summed", "rms_rooted", "merge_read", "out_read",
                 "gu_silu", "hid_done", "hid_hi_done", "hid_lo_done", "hid_turned", "down_done", "down_read",
                 "router_split", "routed", "route_read", "route_exp", "masks_done", "counted", "tables_done", "pick_done",
                 "pick_turned", "pickT_done", "gathered", "hx_hi_done", "hx_lo_done", "oe_hi_done", "oe_lo_done",
                 "scattered", "x_added", "meta_done", "hN_hi_done", "hN_lo_done", "final_done", "ident_done", "pads_done",
                 "extra_done", "router_hi", "xbc_tap", "z_done", "dense_added"]
        S = {n: sem(n) for n in names}

        block = ctx.enter_context(nc.Block())

        MIX_BASE = [0, MIX_PANELS + DENSE_PANELS]
        DENSE_BASE = MIX_PANELS
        EXP_BASE = MIX_BASE[1] + MIX_PANELS

        uses = [0] * FRING
        MSLOT = [[], []]
        DENSE_USE0, EXP_USE0 = None, None
        for L in range(2):
            for i in range(MIX_PANELS):
                s = i % MRING
                MSLOT[L].append((s, uses[s]))
                uses[s] += 1
            if L == 0:
                DENSE_USE0 = list(uses)
                for i in range(DENSE_PANELS):
                    uses[i % FRING] += 1
            else:
                EXP_USE0 = list(uses)
        MREADY = [{}, {}]
        last_user = {}

        def ev(L, name):
            who = CHUNKS[CH_INDEX[name]][2]
            n = sum(1 for c in CHUNKS[:CH_INDEX[name] + 1] if c[2] == who)
            return emptied[who], L * (N_EVA if who == "A" else N_EVD) + n

        def pair_of(name):
            return pairs[CH_INDEX[name] % 2]

        def used_after(L, name):
            return MIX_BASE[L] + CH_PANEL[name] + CHUNKS[CH_INDEX[name]][1]

        def pos_a(s):
            return 3 * s - 1 if not (isinstance(s, int) and s == 0) else 0

        def pos_d(s, n):
            return 3 * n - 1 if isinstance(s, int) and s == n - 1 else 3 * s + 4

        def ffn_span(n):
            return (n - 4) // 2

        @block.sync
        def _(sp):
            sp.dma_start(x[:, :, :], x_d.rearrange("(b p) d -> p b d", p=128)).then_inc(x_in, 16)
            last = {}

            def halves(slot, width, src):
                for h in range(2):
                    sp.dma_start(raw(slot)[:, 2 * h * width:2 * (h + 1) * width].rearrange("p (k n) -> p k n", n=width),
                                 src[:, 2 * h:2 * h + 2, :]).then_inc(raw_in[slot], 16)

            def mixer(L):
                i = 0

                def panel(width, src):
                    nonlocal i
                    slot, _ = MSLOT[L][i]
                    p = MIX_BASE[L] + i
                    if slot in last:
                        sp.wait_ge(lo_ready, last[slot] + 1)
                    halves(slot, width, src)
                    last[slot] = p
                    i += 1

                def chunk_in(c0, width):
                    for kh in range(2):
                        panel(width, w_in[L, kh * 512:(kh + 1) * 512, c0:c0 + width].rearrange("(k p) n -> p k n", p=128))

                for c0, width in ((C_A, 512), (C_GT, 512), (C_KIWI, 40), (C_KVQI, 512), (C_Q, 512), (C_POOL, 512),
                                  (C_XBC0, 512), (C_XBC1, 264), (C_Z, 512)):
                    chunk_in(c0, width)

                def gates(n):
                    for h in range(2):
                        chunk_in(C_GATE + n * D + h * 512, 512)

                def branch(n):
                    for h in range(2):
                        panel(512, w_br[L, n, :, h * 512:(h + 1) * 512].rearrange("(k p) n -> p k n", p=128))

                gates(0)
                branch(0)
                gates(2)
                branch(2)
                gates(1)
                branch(1)
                gates(3)
                branch(3)
                for h in range(2):
                    for kh in range(2):
                        panel(512, w_out[L, kh * 512:(kh + 1) * 512, h * 512:(h + 1) * 512].rearrange("(k p) n -> p k n", p=128))

            def ffn_panel(p, slot, dst_src):
                sp.wait_ge(lo_ready, p - (FRING - 1))
                for dst, src in dst_src:
                    sp.dma_start(dst, src).then_inc(raw_in[slot], 16)

            def ffn_stream(base, n, wg, wu, wd):
                def up(s0, i):
                    for kh in range(2):
                        c = (3 * s0 - 1 if s0 else 0) + kh
                        slot = c % FRING
                        v = raw(slot).rearrange("p (k n) -> p k n", n=512)
                        s = s0 + 2 * i
                        ffn_panel(base + c + 6 * i, slot,
                                  ((v[:, :, 0:STEP_F], wg(kh, s)), (v[:, :, STEP_F:512], wu(kh, s))))

                def down(s0, i):
                    c = 3 * n - 1 if s0 == n - 1 else 3 * s0 + 4
                    slot = c % FRING
                    v = raw(slot).rearrange("p (k n) -> p k n", n=D)
                    src = wd(s0 + 2 * i)
                    ffn_panel(base + c + 6 * i, slot, ((v[:, 0:1, :], src[:, 0:1, :]), (v[:, 1:2, :], src[:, 1:2, :])))

                up(0, 0)
                up(1, 0)
                down(0, 0)
                reps = ffn_span(n)
                with sp.Fori(0, reps) as i:
                    for u in (2, 3):
                        up(u, i)
                        down(u - 1, i)
                for s in range(2 + 2 * reps, n):
                    up(s, 0)
                    down(s - 1, 0)
                down(n - 1, 0)

            mixer(0)
            sp.wait_ge(lo_ready, DENSE_BASE)
            sp.wait_ge(*ev(0, "br3h1"))
            ffn_stream(DENSE_BASE, DENSE_STEPS,
                       lambda kh, s: fg[kh * 512:(kh + 1) * 512, bass.ds(s * STEP_F, STEP_F)].rearrange("(k p) n -> p k n", p=128),
                       lambda kh, s: fu[kh * 512:(kh + 1) * 512, bass.ds(s * STEP_F, STEP_F)].rearrange("(k p) n -> p k n", p=128),
                       lambda s: fd[bass.ds(s * STEP_F, STEP_F), :].rearrange("(k p) n -> p k n", p=128))
            for i in range(DENSE_PANELS):
                last[i % FRING] = DENSE_BASE + i
            mixer(1)
            sp.wait_ge(lo_ready, EXP_BASE)
            sp.wait_ge(*ev(1, "br3h1"))

            def expert(j, e):
                def rows(w, kh, s):
                    return w[bass.ds(e, 1), kh * 512:(kh + 1) * 512, bass.ds(s * STEP_F, STEP_F)].rearrange("a (k p) n -> p (a k) n", p=128)
                ffn_stream(EXP_BASE + j * EXP_PANELS, EXP_STEPS,
                           lambda kh, s: rows(mg, kh, s), lambda kh, s: rows(mu, kh, s),
                           lambda s: md[bass.ds(e, 1), bass.ds(s * STEP_F, STEP_F), :].rearrange("a (k p) n -> p (a k) n", p=128))

            with sp.Fori(0, NE) as j:
                expert(j, j)
            sp.wait_ge(S["meta_done"], 1)
            m = sp.value_load(meta[0:1, 0:1], min_val=0, max_val=EXTRA)
            with sp.If(m > 0):
                with sp.Fori(NE, m + NE) as j:
                    expert(j, sp.value_load(meta[0:1, bass.ds(j - (NE - 1), 1)], min_val=0, max_val=NE - 1))

            sp.wait_ge(S["final_done"], 2)
            sp.dma_start(out_d.rearrange("(b p) d -> p b d", p=128), hN).then_inc(stored, 16)
            sp.wait_ge(stored, 16)

        @block.gpsimd
        def _(pool):
            pool.dma_start(consts[:, :], consts_d).then_inc(const_in, 16)
            pool.dma_start(params[:, :], params_d[0, :, :]).then_inc(param_in, 16)
            for n in range(5):
                if n:
                    pool.wait_ge(S["normed"], 2 * n)
                pool.dma_start(gain[:, :], gains_d[n:n + 1, :].broadcast_to([128, D])).then_inc(gain_in, 16)
                if n == 1:
                    pool.wait_ge(*ev(0, "br3h1"))
                    pool.dma_start(params[:, :], params_d[1, :, :]).then_inc(param_in, 16)

        @block.scalar
        def _(act):
            own = [0]

            def link(ins):
                own[0] += 1
                ins.then_inc(a_done, 1)
                act.wait_ge(a_done, own[0])

            def to_hi(p, slot, use, cols, h=None):
                act.wait_ge(raw_in[slot], 32 * (use + 1))
                if not (isinstance(p, int) and p < HRING):
                    act.wait_ge(panel_used, p - (HRING - 1))
                nc.scalar.activation(hi_ring[:, h, 0:cols], raw(slot)[:, 0:cols], ACT.Copy).then_inc(hi_ready, 1)

            MCOLS = mixer_cols()

            def norm(n):
                for b in range(NB):
                    if n == 0 and b == 0:
                        act.wait_ge(x_in, 16)
                    if n and b == 0:
                        act.wait_ge(*{1: ev(0, "out1"), 2: (S["dense_added"], 1), 3: ev(1, "out1")}[n])
                    nc.scalar.activation(hN[:, b, :], x[:, b, :], ACT.Square,
                                         accum_out=small[:, b:b + 1]).then_inc(S["squared"], 1)
                act.wait_ge(S["meaned"], n + 1)
                nc.scalar.activation(small[:, 4:6], small[:, 2:4], ACT.Sqrt).then_inc(S["rooted"], 1)

            def norm_hi(n):
                for j in range(4):
                    act.wait_ge(S["turned"], 4 * n + j + 1)
                    nc.scalar.activation(hT_hi[:, 2 * j:2 * j + 2, :].rearrange("p k t -> p (k t)"),
                                         aux[:, j * 512:(j + 1) * 512], ACT.Copy).then_inc(S["hT_hi_done"], 1)

            def mixer(L):
                done = [0]

                def hi_upto(n):
                    while done[0] < min(n, MIX_PANELS):
                        i = done[0]
                        slot, use = MSLOT[L][i]
                        p = MIX_BASE[L] + i
                        to_hi(p, slot, use, MCOLS[i], p % HRING)
                        done[0] += 1

                def after(name):
                    hi_upto(CH_PANEL[name] + CHUNKS[CH_INDEX[name]][1] + 2)
                    act.wait_ge(panel_used, used_after(L, name))

                def evac(out, in_, func=ACT.Copy, scale=1.0, last=False):
                    ins = nc.scalar.activation(out, in_, func, scale=scale)
                    if last:
                        ins.then_inc(emptied["A"], 1)

                if L:
                    act.wait_ge(S["pads_done"], L + 1)
                else:
                    act.wait_ge(const_in, 16)
                    nc.scalar.activation(ident_r[:, :], C("ident"), ACT.Copy).then_inc(S["ident_done"], 1)
                norm(2 * L)
                hi_upto(3)
                norm_hi(2 * L)
                after("a")
                evac(ar(A_P, 1024), pair_of("a")[:, :], last=True)
                after("gt")
                evac(ar(A_P + 1024, 1024), pair_of("gt")[:, :], ACT.Sigmoid, last=True)
                after("kiwi")
                g = pair_of("kiwi")
                for b in range(NB):
                    evac(ar3(A_KI + b * 128, 4, 32), g[:, b * 40:b * 40 + 32].unsqueeze(1).broadcast_to([128, 4, 32]))
                    evac(ar(A_MISC + b * 8, 8), g[:, b * 40 + 32:b * 40 + 40], last=(b == NB - 1))
                after("kvqi")
                g = pair_of("kvqi")
                evac(ar(A_QK + 1024, 256), g[:, 0:256])
                evac(ar(A_V, 256), g[:, 256:512])
                evac(ar(A_IDX, 512), g[:, 512:1024], last=True)
                after("q")
                evac(ar(A_QK, 1024), pair_of("q")[:, :], last=True)
                after("pool")
                evac(ar3(A_UPAD, 4, PPAD + T)[:, :, PPAD:], pair_of("pool")[:, :].rearrange("p (g t) -> p g t", t=T), last=True)
                act.wait_ge(S["ki_turned"], L + 1)
                nc.scalar.activation(ar(A_IDX + 512, 256), aux[:, 0:256], ACT.Copy).then_inc(S["ki_copied"], 1)
                after("xbc0")
                evac(ar3(A_XBCP, 6, SPAD + T)[:, 0:4, SPAD:], pair_of("xbc0")[:, :].rearrange("p (g t) -> p g t", t=T), last=True)
                after("xbc1")
                g = pair_of("xbc1")
                evac(ar3(A_XBCP, 6, SPAD + T)[:, 4:6, SPAD:], g[:, 0:512].rearrange("p (g t) -> p g t", t=T))
                evac(ar(A_MISC + 16, 16), g[:, 512:528], last=True)
                after("z")
                evac(ar(A_Z, 1024), pair_of("z")[:, :], last=True)

                def gates(n):
                    for h in range(2):
                        name = f"g{n}h{h}"
                        after(name)
                        evac(ar(A_GATES + h * 1024, 1024), pair_of(name)[:, :], ACT.Sigmoid, last=True)

                def branch_hi(i):
                    nc.scalar.activation(act_hi[:, (i % 2) * 1024:(i % 2 + 1) * 1024], ar(A_UPAD, 1024), ACT.Copy)\
                       .then_inc(S["branch_hi"], 1)

                def relu(b):
                    act.wait_ge(S["indexed"], 2 * L + b + 1)
                    if b == 0:
                        act.wait_ge(S["pooled"], L + 1)
                    else:
                        act.wait_ge(S["scored"], 2 * L + b)
                    w = 128 * (b + 1)
                    nc.scalar.activation(ar3(A_P, 8, w).rearrange("p (h j) w -> p j h w", j=4),
                                         aux[:, :].rearrange("p (j c) -> p j c", j=4)[:, :, 0:2 * w]
                                         .rearrange("p j (h w) -> p j h w", w=w), ACT.Relu).then_inc(S["relued"], 1)

                gates(0)
                act.wait_ge(S["k_swapped"], L + 1)
                nc.scalar.activation(ar(A_KI, 256), aux[:, 0:256], ACT.Copy).then_inc(S["k_copied"], 1)
                relu(0)
                act.wait_ge(S["pool_mixed"], L + 1)
                for g in range(MG):
                    ins = nc.scalar.activation(ar(A_UPAD + g * T, T), pair_of("pooly")[:, g * T:(g + 1) * T], ACT.Copy,
                                               scale=W("pool_scale", g))
                ins.then_inc(emptied["A"], 1)
                act.wait_ge(*ev(L, "pooly"))
                branch_hi(0)
                hi_upto(26)
                act.wait_ge(S["centred"], L + 1)
                nc.scalar.activation(ar(A_P, 1024), ar(A_CACC, 1024), ACT.Square).then_inc(S["ln_squared"], 1)
                after("g2h0")
                act.wait_ge(*ev(L, "br0h1"))
                evac(ar(A_GATES, 1024), pair_of("g2h0")[:, :], ACT.Sigmoid, last=True)
                hi_upto(CH_PANEL["g2h1"] + 1)
                act.wait_ge(*ev(L, "lnvar"))
                nc.scalar.activation(ar(A_MISC + 128, T), ar(A_MISC + 128, T), ACT.Sqrt).then_inc(S["ln_rooted"], 1)
                after("g2h1")
                evac(ar(A_GATES + 1024, 1024), pair_of("g2h1")[:, :], ACT.Sigmoid, last=True)
                act.wait_ge(S["ln_scaled"], L + 1)
                for g in range(MG):
                    ins = nc.scalar.activation(ar(A_P + g * T, T), ar(A_CACC + g * T, T), ACT.Sigmoid,
                                               scale=W("ln_g", g), bias=W("ln_b", g))
                ins.then_inc(S["ln_sig"], 1)
                act.wait_ge(S["branch_f"], 2 * L + 1)
                branch_hi(1)
                relu(1)
                act.wait_ge(S["dt_abs"], L + 1)
                nc.scalar.activation(ar(A_MISC + 48, 16), ar(A_MISC + 48, 16), ACT.Exp, scale=-1.0).then_inc(S["dt_exp"], 1)
                nc.scalar.activation(ar(A_MISC + 112, 8), W("a_log", 0, 8), ACT.Exp).then_inc(S["a_exp"], 1)
                act.wait_ge(S["dt_plus"], L + 1)
                nc.scalar.activation(ar(A_MISC + 80, 16), ar(A_MISC + 64, 16), ACT.Ln).then_inc(S["dt_ln"], 1)

                def exps(u):
                    j, b = u // 2, u % 2
                    w = 128 * (b + 1)
                    act.wait_ge(S["negmax_done"], 8 * L + u + 1)
                    for r in range(2):
                        ins = nc.scalar.activation(ar(A_CACC + 512 + r * 256, w), ar(A_CACC + r * 256, w), ACT.Exp,
                                                   bias=ar(A_MISC + 96 + r, 1), accum_out=ar(A_MISC + 98 + r, 1))
                    ins.then_inc(S["exped"], 1)

                def probs_out(u):
                    j, b = u // 2, u % 2
                    act.wait_ge(S["probs_turned"], 8 * L + u + 1)
                    n = 2 * (b + 1) * 128
                    nc.scalar.activation(ar(A_YPAD, n), aux[:, 1024:1024 + n], ACT.Copy).then_inc(S["probs_copied"], 1)
                    if b == 1:
                        act.wait_ge(S["attended"], 8 * L + u + 1)
                        nc.scalar.activation(ar(A_UPAD + j * T, T), aux[:, 1536 + (j % 2) * 256:1536 + (j % 2) * 256 + 256],
                                             ACT.Copy).then_inc(S["att_copied"], 1)

                act.wait_ge(S["branch_lo"], 4 * L + 2)
                for u in range(8):
                    hi_upto(28 + u + 2 if u < 6 else 36)
                    exps(u)
                    hi_upto(28 + u + 3 if u < 6 else 36)
                    probs_out(u)
                    if u == 3:
                        act.wait_ge(*ev(L, "br2h1"))
                        after("g1h0")
                        evac(ar(A_GATES, 1024), pair_of("g1h0")[:, :], ACT.Sigmoid, last=True)
                    if u == 5:
                        after("g1h1")
                        evac(ar(A_GATES + 1024, 1024), pair_of("g1h1")[:, :], ACT.Sigmoid, last=True)
                act.wait_ge(S["att_copied"], 4 * (L + 1))
                branch_hi(2)
                act.wait_ge(S["xbc_tap"], 24 * (L + 1))
                nc.scalar.activation(ar(A_P, 1536), ar(A_XBC, 1536), ACT.Sigmoid).then_inc(S["xbc_sig"], 1)
                act.wait_ge(S["branch_lo"], 4 * L + 3)
                nc.scalar.activation(ar(A_UPAD, 1024), ar(A_Z, 1024), ACT.Sigmoid).then_inc(S["z_sig"], 1)
                hi_upto(38)

                def decay(h):
                    act.wait_ge(S["arow_read"], 8 * L + h + 1)
                    e = A_YPAD + (h % 2) * 384
                    nc.scalar.activation(ar(e, 384), ar(e, 384), ACT.Exp).then_inc(S["decay_exp"], 1)

                for h in range(8):
                    if h % 2 == 0:
                        hi_upto(36 + h // 2 + 3)
                    decay(h)
                after("g3h0")
                act.wait_ge(*ev(L, "br1h1"))
                evac(ar(A_GATES, 1024), pair_of("g3h0")[:, :], ACT.Sigmoid, last=True)
                after("g3h1")
                evac(ar(A_GATES + 1024, 1024), pair_of("g3h1")[:, :], ACT.Sigmoid, last=True)
                act.wait_ge(S["gated"], L + 1)
                nc.scalar.activation(ar(A_P, 1024), ar(A_XBCP, 1024), ACT.Square).then_inc(S["rms_squared"], 1)
                act.wait_ge(*ev(L, "rmsum"))
                nc.scalar.activation(ar(A_MISC + 128, T), ar(A_MISC + 128, T), ACT.Sqrt).then_inc(S["rms_rooted"], 1)
                act.wait_ge(S["branch_f"], 2 * L + 2)
                branch_hi(3)
                hi_upto(MIX_PANELS - 1)
                for h in range(2):
                    act.wait_ge(*ev(L, f"br3h{h}"))
                    if h == 0:
                        act.wait_ge(panel_used, used_after(L, "br3h1"))
                    nc.scalar.activation(act_hi[:, h * 1024:(h + 1) * 1024], mrg[:, h * 1024:(h + 1) * 1024], ACT.Copy)\
                       .then_inc(S["merged_hi"], 1)
                hi_upto(MIX_PANELS)

            def ffn_stream(base, use0, n, silu, hid_hi_op, start=lambda: None, middle=lambda: None, before_last=lambda: None):
                def hi(c, i):
                    slot = c % FRING
                    to_hi(base + c + 6 * i, slot, use0(slot) + c // FRING + i, PANEL, (BASE_MOD[0] + c) % HRING)

                def step(s0, i):
                    silu(s0, i)
                    if s0 < n - 1:
                        hi(3 * s0 + 3, i)
                        if s0 == 1:
                            middle()
                        hid_hi_op(s0, i)
                        hi(3 * s0 + 4, i)
                        if s0 < n - 2:
                            hi(3 * s0 + 5, i)
                    else:
                        hi(3 * n - 1, i)
                        before_last()
                        hid_hi_op(s0, i)

                hi(0, 0)
                hi(1, 0)
                start()
                hi(2, 0)
                step(0, 0)
                step(1, 0)
                reps = ffn_span(n)
                with act.Fori(0, reps) as i:
                    for u in (2, 3):
                        step(u, i)
                for s in range(2 + 2 * reps, n):
                    step(s, 0)

            BASE_MOD = [0]

            mixer(0)
            norm(1)
            norm_hi(1)

            def dense_silu(s0, i):
                c = (3 * s0 - 1 if s0 else 0) + 2
                act.wait_ge(panel_used, DENSE_BASE + c + 6 * i)
                if s0 >= 2:
                    act.wait_ge(S["hid_done"], s0 + 2 * i - 1)
                nc.scalar.activation(ar(A_SG + (s0 % 2) * 512, 512), pairs[s0 % 2][:, 0:512], ACT.Silu).then_inc(S["gu_silu"], 1)

            def dense_hid_hi(s0, i):
                act.wait_ge(S["hid_done"], s0 + 2 * i + 1)
                if s0 >= 2:
                    act.wait_ge(panel_used, DENSE_BASE + 3 * (s0 - 2) + 4 + 6 * i + 1)
                o = (s0 % 2) * 512
                nc.scalar.activation(act_hi[:, o:o + 512], ar(A_HID + o, 512), ACT.Copy).then_inc(S["hid_hi_done"], 1)

            BASE_MOD[0] = DENSE_BASE % HRING
            ffn_stream(DENSE_BASE, lambda s: DENSE_USE0[s], DENSE_STEPS, dense_silu, dense_hid_hi)

            mixer(1)
            norm(3)
            norm_hi(3)
            act.wait_ge(S["normed"], 8)
            nc.scalar.activation(act_hi[:, :], mrg[:, :], ACT.Copy).then_inc(S["hN_hi_done"], 1)
            act.wait_ge(param_in, 32)
            nc.scalar.activation(rt_hi[:, :], W("router", 0, 64), ACT.Copy).then_inc(S["router_hi"], 1)
            act.wait_ge(S["route_read"], 1)
            nc.scalar.activation(small[:, 12:14], small[:, 10:12], ACT.Exp).then_inc(S["route_exp"], 1)

            def hx_hi(j):
                act.wait_ge(S["gathered"], j + 1)
                nc.scalar.activation(hT_hi[:, 0:4, :].rearrange("p k t -> p (k t)"), aux[:, 1024:2048], ACT.Copy)\
                   .then_inc(S["hx_hi_done"], 1)

            def expert(j, first=False):
                base = EXP_BASE + j * EXP_PANELS
                d0 = DENSE_STEPS + j * EXP_STEPS

                def silu(s0, i):
                    c = (3 * s0 - 1 if s0 else 0) + 2
                    act.wait_ge(panel_used, base + c + 6 * i)
                    act.wait_ge(S["hid_done"], d0 + s0 + 2 * i - 1)
                    nc.scalar.activation(ar(A_SG + (s0 % 2) * 512, STEP_F), pairs[s0 % 2][:, 0:STEP_F], ACT.Silu)\
                       .then_inc(S["gu_silu"], 1)

                def hid_hi_op(s0, i):
                    act.wait_ge(S["hid_turned"], j * EXP_STEPS + s0 + 2 * i + 1)
                    if s0 >= 2:
                        act.wait_ge(panel_used, base + 3 * (s0 - 2) + 5 + 6 * i)
                    nc.scalar.activation(hid_hi[:, s0 % 2, :], pairs[s0 % 2][:, 512:512 + STEP_F], ACT.Copy)\
                       .then_inc(S["hid_hi_done"], 1)

                def pickT_copy():
                    act.wait_ge(S["pick_turned"], j + 1)
                    nc.scalar.activation(pickT[:, :, :].rearrange("p b t -> p (b t)"), aux[:, 1024:1280], ACT.Copy)\
                       .then_inc(S["pickT_done"], 1)

                ffn_stream(base, lambda s: EXP_USE0[s] + (EXP_PANELS // FRING) * j, EXP_STEPS, silu, hid_hi_op,
                           (lambda: None) if first else (lambda: output_hi(j - 1)), pickT_copy, lambda: hx_hi(j + 1))

            def output_hi(j):
                act.wait_ge(panel_used, EXP_BASE + (j + 1) * EXP_PANELS)
                nc.scalar.activation(hT_hi[:, 4:8, :].rearrange("p k t -> p (k t)"), aux[:, 0:1024], ACT.Copy)\
                   .then_inc(S["oe_hi_done"], 1)

            BASE_MOD[0] = EXP_BASE % HRING
            hx_hi(0)
            expert(0, True)
            with act.Fori(1, NE) as j:
                expert(j)
            act.wait_ge(S["meta_done"], 1)
            m = act.value_load(meta[0:1, 0:1], min_val=0, max_val=EXTRA)
            with act.If(m > 0):
                with act.Fori(NE, m + NE) as j:
                    expert(j)
            output_hi(m + (NE - 1))
            act.wait_ge(S["extra_done"], 1)
            for b in range(NB):
                nc.scalar.activation(hN[:, b, :], x[:, b, :], ACT.Square, accum_out=small[:, b:b + 1]).then_inc(S["squared"], 1)
            act.wait_ge(S["meaned"], 5)
            nc.scalar.activation(small[:, 4:6], small[:, 2:4], ACT.Sqrt).then_inc(S["rooted"], 1)

        @block.tensor
        def _(pe):
            def passes(hi, lo, rhi, rlo):
                return ((hi, rlo), (lo, rhi), (hi, rhi))

            def split_mm(out, a, b, first, last=False):
                for n, (l, r) in enumerate(((a[0], b[1]), (a[1], b[0]), (a[0], b[0]))):
                    ins = pe.matmul(out, l, r, start=first and n == 0, stop=last and n == 2, skip_group_check=True)
                return ins

            def weights(h, width):
                return (hi_ring[:, h, 0:4 * width].rearrange("p (k n) -> p k n", n=width),
                        lo_ring[:, h, 0:4 * width].rearrange("p (k n) -> p k n", n=width))

            def norm(n):
                for j in range(4):
                    if j == 0:
                        if n == 0:
                            pe.wait_ge(const_in, 16)
                        pe.wait_ge(S["normed"], 2 * n + 2)
                    for k in range(2 * j, 2 * j + 2):
                        for b in range(NB):
                            o = j * 512 + (k % 2) * 256 + b * 128
                            ins = pe.transpose(aux[:, o:o + 128], hN[:, b, k * 128:(k + 1) * 128], C("ident"))
                    ins.then_inc(S["turned"], 1)

            def mixer(L):
                p = [MIX_BASE[L]]
                norm(2 * L)
                pe.wait_ge(S["hT_lo_done"], 4 * (2 * L + 1))

                def free(name):
                    q = CH_INDEX[name]
                    if q >= 2:
                        pe.wait_ge(*ev(L, CHUNKS[q - 2][0]))

                def panel(width, body):
                    pe.wait_ge(lo_ready, p[0] + 1)
                    body(weights(p[0] % HRING, width)).then_inc(panel_used, 1)
                    p[0] += 1

                def t_block(out, w, c0, kh, first):
                    for k in range(4):
                        ins = split_mm(out, (w[0][:, k, c0:c0 + 128], w[1][:, k, c0:c0 + 128]),
                                       (hT_hi[:, 4 * kh + k, :], hT_lo[:, 4 * kh + k, :]),
                                       first and k == 0, kh == 1 and k == 3)
                    return ins

                def n_block(out, w, c0, n, b, kh, first):
                    for k in range(4):
                        ins = split_mm(out, (hT_hi[:, 4 * kh + k, b * 128:(b + 1) * 128], hT_lo[:, 4 * kh + k, b * 128:(b + 1) * 128]),
                                       (w[0][:, k, c0:c0 + n], w[1][:, k, c0:c0 + n]), first and k == 0, kh == 1 and k == 3)
                    return ins

                def t_chunk(name, groups=4, width=512):
                    free(name)
                    g = pair_of(name)
                    for kh in range(2):
                        def body(w):
                            for i in range(groups):
                                ins = t_block(g[:, i * T:(i + 1) * T], w, i * 128, kh, kh == 0 and i % 2 == 0)
                            if name == "xbc1":
                                for b in range(NB):
                                    ins = n_block(g[:, 512 + b * 8:520 + b * 8], w, 256, 8, b, kh, kh == 0 and b == 0)
                            return ins
                        panel(width, body)

                t_chunk("a")
                t_chunk("gt")
                free("kiwi")
                for kh in range(2):
                    def body(w):
                        for b in range(NB):
                            ins = n_block(pair_of("kiwi")[:, b * 40:(b + 1) * 40], w, 0, 40, b, kh, kh == 0 and b == 0)
                        return ins
                    panel(40, body)
                free("kvqi")
                for kh in range(2):
                    def body(w):
                        g = pair_of("kvqi")
                        t_block(g[:, 0:256], w, 0, kh, kh == 0)
                        for b in range(NB):
                            n_block(g[:, 256 + b * 128:384 + b * 128], w, 128, 128, b, kh, False)
                        t_block(g[:, 512:768], w, 256, kh, kh == 0)
                        return t_block(g[:, 768:1024], w, 384, kh, False)
                    panel(512, body)
                t_chunk("q")
                t_chunk("pool")
                pe.wait_ge(*ev(L, "kiwi"))
                pe.wait_ge(S["hT_lo_done"], 4 * (2 * L + 1))
                for b in range(NB):
                    ins = pe.transpose(aux[:, b * 128:(b + 1) * 128], ar(A_KI + b * 128, 128), C("ident"))
                ins.then_inc(S["ki_turned"], 1)
                t_chunk("xbc0")
                pe.wait_ge(S["ki_copied"], L + 1)
                pe.wait_ge(*ev(L, "q"))
                for i in range(8):
                    src = ar(A_IDX + i * T, T) if i < 3 else ar(A_QK + (i - 3) * T, T)
                    ins = pe.matmul(aux[:, i * T:(i + 1) * T], C("roti") if i < 3 else C("rotq"), src, start=True, stop=True)
                ins.then_inc(S["rotated"], 1)
                t_chunk("xbc1", 2, 264)
                t_chunk("z")
                t_chunk("g0h0")
                t_chunk("g0h1")

                pe.wait_ge(S["roped"], L + 1)
                pe.matmul(aux[:, 0:256], C("swap"), ar(A_QK + 1024, 256), start=True, stop=True).then_inc(S["k_swapped"], 1)

                def index(b):
                    w = 128 * (b + 1)
                    if b == 0:
                        pe.wait_ge(S["k_copied"], L + 1)
                    else:
                        pe.wait_ge(S["relued"], 2 * L + 1)
                    for h in range(8):
                        r = 32 * (h % 4)
                        ins = pe.matmul(aux[:, 512 * (h % 4) + (h // 4) * w:512 * (h % 4) + (h // 4 + 1) * w],
                                        arena[r:r + 32, A_IDX + (h // 4) * T + b * 128:A_IDX + (h // 4) * T + (b + 1) * 128],
                                        arena[r:r + 32, A_IDX + 512:A_IDX + 512 + w], start=True, stop=True)
                    ins.then_inc(S["indexed"], 1)

                index(0)
                free("pooly")
                pe.wait_ge(S["pooled"], L + 1)
                for g in range(MG):
                    o = A_UPAD + g * (PPAD + T) + PPAD
                    ins = pe.matmul(pair_of("pooly")[:, g * T:(g + 1) * T], W("pool_w", g * 128, 128), ar(o, T),
                                    start=True, stop=True)
                ins.then_inc(S["pool_mixed"], 1)

                def branch(i):
                    n = BR_ORDER[i]
                    pe.wait_ge(S["branch_lo"], 4 * L + i + 1)
                    for h in range(2):
                        name = f"br{n}h{h}"
                        free(name)

                        def body(w):
                            for g in range(4):
                                for k in range(4):
                                    o = (i % 2) * 1024 + k * T
                                    ins = split_mm(pair_of(name)[:, g * T:(g + 1) * T],
                                                   (w[0][:, k, g * 128:(g + 1) * 128], w[1][:, k, g * 128:(g + 1) * 128]),
                                                   (act_hi[:, o:o + T], act_lo[:, o:o + T]), k == 0 and g % 2 == 0, k == 3)
                            return ins
                        yield
                        panel(512, body)

                def run(gen):
                    for _ in gen:
                        pass

                run(branch(0))
                index(1)
                free("lnsum")
                pe.wait_ge(S["conved"], 4 * CONV_W * (L + 1))
                for g in range(MG):
                    ins = pe.matmul(pair_of("lnsum")[:, 0:T], C("ones"), ar(A_CACC + g * T, T), start=(g == 0), stop=(g == 3))
                ins.then_inc(S["ln_summed"], 1)
                t_chunk("g2h0")
                free("lnvar")
                pe.wait_ge(S["ln_squared"], L + 1)
                for g in range(MG):
                    ins = pe.matmul(pair_of("lnvar")[:, 0:T], C("ones"), ar(A_P + g * T, T), start=(g == 0), stop=(g == 3))
                ins.then_inc(S["ln_varied"], 1)
                t_chunk("g2h1")

                def logits(u):
                    j, b = u // 2, u % 2
                    w = 128 * (b + 1)
                    pe.wait_ge(S["relued"], 2 * L + 2)
                    if u:
                        pe.wait_ge(S["logits_read"], 8 * L + u)
                    for r in range(2):
                        kv = j // 2
                        ko = A_QK + 1024 if kv == r else A_KI
                        ins = pe.matmul(aux[:, r * 512:r * 512 + w],
                                        arena[64 * r:64 * r + 64, A_QK + j * T + b * 128:A_QK + j * T + (b + 1) * 128],
                                        arena[64 * r:64 * r + 64, ko:ko + w], start=True, stop=True)
                    ins.then_inc(S["logits_done"], 1)

                def attend(u):
                    j, b = u // 2, u % 2
                    nb = b + 1
                    pe.wait_ge(S["probs_done"], 8 * L + u + 1)
                    for r in range(2):
                        for s in range(nb):
                            o = 1024 + (r * nb + s) * 128
                            ins = pe.transpose(aux[:, o:o + 128], ar(A_CACC + 512 + r * 256 + s * 128, 128), C("ident"))
                    ins.then_inc(S["probs_turned"], 1)
                    pe.wait_ge(S["probs_copied"], 8 * L + u + 1)
                    if b == 0 and j:
                        pe.wait_ge(S["att_copied"], 4 * L + j)
                    o = 1536 + (j % 2) * 256 + b * 128
                    for r in range(2):
                        for s in range(nb):
                            v = ar(A_V + s * 128 + (j // 2) * 64, 64)
                            ins = pe.matmul(aux[64 * r:64 * r + 64, o:o + 128], v, ar(A_YPAD + (r * nb + s) * 128, 128),
                                            start=(s == 0), stop=(s == nb - 1))
                    ins.then_inc(S["attended"], 1)

                logits(0)
                b2 = branch(1)
                next(b2)
                next(b2)
                attend(0)
                logits(1)
                run(b2)
                attend(1)

                def t_halves(name):
                    free(name)
                    g = pair_of(name)
                    for kh in range(2):
                        def body(w):
                            for i in range(4):
                                ins = t_block(g[:, i * T:(i + 1) * T], w, i * 128, kh, kh == 0 and i % 2 == 0)
                            return ins
                        yield
                        panel(512, body)

                u = 2
                for name in ("g1h0", "g1h1"):
                    gen = t_halves(name)
                    next(gen)
                    for kh in range(2):
                        logits(u)
                        next(gen, None)
                        attend(u)
                        u += 1
                for u in (6, 7):
                    logits(u)
                    attend(u)
                run(branch(2))

                pe.wait_ge(S["xbc_done"], L + 1)
                for b in range(NB):
                    for g in range(MG):
                        ins = pe.transpose(aux[:, b * 512 + g * 128:b * 512 + (g + 1) * 128],
                                           ar(A_XBC + g * T + b * 128, 128), C("ident"))
                ins.then_inc(S["xs_turned"], 1)
                pe.wait_ge(S["att_copied"], 4 * (L + 1))
                for g in range(2):
                    r, o = 64 * g, 1024 + 512 * g
                    bT, cT = A_XBC + 4 * T, A_XBC + 5 * T
                    pe.matmul(aux[:, o:o + 256], arena[r:r + 64, bT:bT + 128], arena[r:r + 64, cT:cT + 256], start=True, stop=True)
                    ins = pe.matmul(aux[:, o + 256:o + 384], arena[r:r + 64, bT + 128:bT + 256],
                                    arena[r:r + 64, cT + 128:cT + 256], start=True, stop=True)
                ins.then_inc(S["cb_done"], 1)
                da = ar3(A_MISC + 32, 2, 8)
                pe.wait_ge(S["dt_done"], L + 1)
                pe.wait_ge(S["xd_done"], L + 1)
                pe.matmul(aux[:, 0:8], C("tri"), da[:, 0, :], start=True, stop=True)
                pe.matmul(aux[:, 8:16], C("ones"), da[:, 0, :], start=True, stop=False)
                pe.matmul(aux[:, 8:16], C("tri"), da[:, 1, :], start=False, stop=True).then_inc(S["acol_done"], 1)

                def arows(g):
                    if g == 0:
                        pe.wait_ge(S["acol_read"], L + 1)
                    else:
                        pe.wait_ge(S["arow_read"], 8 * L + 4)
                    for i in range(4):
                        h = 4 * g + i
                        o = i * 256
                        pe.matmul(aux[:, o:o + 256], da[:, 0, h:h + 1].broadcast_to([128, 128]),
                                  consts[:, CONSTS["tri"][0]:CONSTS["tri"][0] + 256], start=True, stop=False)
                        ins = pe.matmul(aux[:, o + 128:o + 256], da[:, 1, h:h + 1].broadcast_to([128, 128]), C("tri"),
                                        start=False, stop=True)
                    ins.then_inc(S["arow_done"], 1)

                def yhead(h):
                    pe.wait_ge(S["mixm_done"], 8 * L + h + 1)
                    if h == 0:
                        pe.wait_ge(S["cbm_done"], L + 1)
                    r, o = 64 * (h % 2), 1024 + (h // 2) * 256
                    m = A_P + 1024 + (h % 2) * 384
                    pe.matmul(aux[r:r + 64, o:o + 256], ar(A_P + h * 64, 64), ar(m, 256), start=True, stop=False)
                    ins = pe.matmul(aux[r:r + 64, o + 128:o + 256], ar(A_P + 512 + h * 64, 64), ar(m + 256, 128),
                                    start=False, stop=True)
                    ins.then_inc(S["y_done"], 1)

                arows(0)
                gens = []
                h = 0
                for name in ("g3h0", "g3h1"):
                    gen = t_halves(name)
                    next(gen)
                    for kh in range(2):
                        next(gen, None)
                        if h == 2:
                            arows(1)
                        yhead(h)
                        yhead(h + 1)
                        h += 2
                free("rmsum")
                pe.wait_ge(S["rms_squared"], L + 1)
                for g in range(MG):
                    ins = pe.matmul(pair_of("rmsum")[:, 0:T], C("ones"), ar(A_P + g * T, T), start=(g == 0), stop=(g == 3))
                ins.then_inc(S["rms_summed"], 1)
                run(branch(3))
                for h in range(2):
                    name = f"out{h}"
                    free(name)
                    for kh in range(2):
                        pe.wait_ge(S["merged_lo"], 2 * L + kh + 1)

                        def body(w):
                            for b in range(NB):
                                for k in range(4):
                                    o = (4 * kh + k) * T + b * 128
                                    ins = split_mm(pair_of(name)[:, b * 512:(b + 1) * 512],
                                                   (act_hi[:, o:o + 128], act_lo[:, o:o + 128]),
                                                   (w[0][:, k, :], w[1][:, k, :]), kh == 0 and k == 0, kh == 1 and k == 3)
                            return ins
                        panel(512, body)

            def ffn_stream(n, up, down, turn, after_b0=lambda: None, after_a1=lambda: None, after_d0=lambda: None):
                def step(s0, i):
                    up(s0, i, 0)
                    if s0 == 1:
                        after_a1()
                    up(s0, i, 1)
                    if s0 == 0:
                        after_b0()
                    else:
                        down(s0 - 1, i)
                    if s0 == 1:
                        after_d0()
                    if s0 < n - 1:
                        turn(s0, i)

                step(0, 0)
                step(1, 0)
                reps = ffn_span(n)
                with pe.Fori(0, reps) as i:
                    for u in (2, 3):
                        step(u, i)
                for s in range(2 + 2 * reps, n):
                    step(s, 0)

            mixer(0)
            norm(1)
            pe.wait_ge(S["hT_lo_done"], 8)

            def dense_up(s0, i, kh):
                c = (3 * s0 - 1 if s0 else 0) + kh
                if kh == 0 and s0 >= 2:
                    pe.wait_ge(S["hid_done"], s0 + 2 * i - 1)
                pe.wait_ge(lo_ready, DENSE_BASE + c + 6 * i + 1)
                w = weights((DENSE_BASE + c) % HRING, 512)
                for g in range(4):
                    for k in range(4):
                        ins = split_mm(pairs[s0 % 2][:, g * T:(g + 1) * T],
                                       (w[0][:, k, g * 128:(g + 1) * 128], w[1][:, k, g * 128:(g + 1) * 128]),
                                       (hT_hi[:, 4 * kh + k, :], hT_lo[:, 4 * kh + k, :]), kh == 0 and k == 0 and g % 2 == 0,
                                       kh == 1 and k == 3)
                ins.then_inc(panel_used, 1)

            def dense_down(s0, i):
                c = DENSE_PANELS - 1 if s0 == DENSE_STEPS - 1 else 3 * s0 + 4
                pe.wait_ge(S["hid_lo_done"], s0 + 2 * i + 1)
                pe.wait_ge(lo_ready, DENSE_BASE + c + 6 * i + 1)
                w = weights((DENSE_BASE + c) % HRING, D // 2)
                o = (s0 % 2) * 512
                for b in range(NB):
                    for half in range(2):
                        for k in range(2):
                            q = o + k * T + b * 128
                            ins = split_mm(aux[:, (2 * b + half) * 512:(2 * b + half + 1) * 512],
                                           (act_hi[:, q:q + 128], act_lo[:, q:q + 128]),
                                           (w[0][:, 2 * k + half, :], w[1][:, 2 * k + half, :]),
                                           s0 == 0 and k == 0, s0 == DENSE_STEPS - 1 and k == 1)
                ins.then_inc(panel_used, 1)

            ffn_stream(DENSE_STEPS, dense_up, dense_down, lambda s0, i: None)
            dense_down(DENSE_STEPS - 1, 0)

            mixer(1)
            norm(3)
            pe.wait_ge(S["hT_lo_done"], 16)
            pe.wait_ge(S["router_split"], 1)
            for b in range(NB):
                for k in range(KT):
                    hs = (hT_lo[:, k, b * 128:(b + 1) * 128], hT_hi[:, k, b * 128:(b + 1) * 128])
                    for n, (l, r) in enumerate(((hs[0], rt_lo), (hs[0], rt_hi), (hs[1], rt_lo), (hs[1], rt_hi))):
                        ins = pe.matmul(aux[:, b * 8:b * 8 + 8], l, r[:, k * 8:k * 8 + 8], start=(k == 0 and n == 0),
                                        stop=(k == KT - 1 and n == 3))
            ins.then_inc(S["routed"], 1)
            pe.wait_ge(S["masks_done"], 1)
            m0, m1 = ar(A_SCORE, 8), ar(A_SCORE + 8, 8)
            pe.matmul(aux[:, 512:520], C("strict"), m0, start=True, stop=True)
            pe.matmul(aux[:, 520:528], C("ones"), m0, start=True, stop=False)
            pe.matmul(aux[:, 520:528], C("strict"), m1, start=False, stop=True)
            pe.matmul(aux[:, 528:536], C("ones"), m0, start=True, stop=False)
            pe.matmul(aux[:, 528:536], C("ones"), m1, start=False, stop=True).then_inc(S["counted"], 1)

            def gather(j):
                pe.wait_ge(S["pick_done"], j + 1)
                for k in range(KT):
                    for b in range(NB):
                        for n, src in enumerate((act_lo, act_hi)):
                            ins = pe.matmul(aux[:, 1024 + k * 128:1024 + (k + 1) * 128], src[:, b * D + k * 128:b * D + (k + 1) * 128],
                                            pick[:, b, :], start=(b == 0 and n == 0), stop=(b == 1 and n == 1))
                ins.then_inc(S["gathered"], 1)

            def expert(j, first=False):
                base = EXP_BASE + j * EXP_PANELS
                d0 = DENSE_STEPS + j * EXP_STEPS

                def up(s0, i, kh):
                    c = (3 * s0 - 1 if s0 else 0) + kh
                    if kh == 0:
                        pe.wait_ge(S["hid_lo_done"], d0 + s0 + 2 * i - 1)
                    pe.wait_ge(lo_ready, base + c + 6 * i + 1)
                    w = weights((EXP_BASE + c) % HRING, 512)
                    for k in range(4):
                        a = (4 * kh + k) * 128
                        ins = split_mm(pairs[s0 % 2][:, 0:512], (hxh[:, a:a + 128], hxl[:, a:a + 128]),
                                       (w[0][:, k, :], w[1][:, k, :]), kh == 0 and k == 0, kh == 1 and k == 3)
                    ins.then_inc(panel_used, 1)

                def turn(s0, i):
                    pe.wait_ge(S["hid_done"], d0 + s0 + 2 * i + 1)
                    for k in range(2):
                        ins = pe.transpose(pairs[s0 % 2][:, 512 + k * 128:640 + k * 128],
                                           ar(A_HID + (s0 % 2) * 512 + k * 128, 128), C("ident"))
                    ins.then_inc(S["hid_turned"], 1)

                def down(s0, i):
                    c = EXP_PANELS - 1 if s0 == EXP_STEPS - 1 else 3 * s0 + 4
                    pe.wait_ge(S["hid_lo_done"], d0 + s0 + 2 * i + 1)
                    pe.wait_ge(lo_ready, base + c + 6 * i + 1)
                    w = weights((EXP_BASE + c) % HRING, 512)
                    for half in range(2):
                        for k in range(2):
                            ins = split_mm(aux[:, half * 512:(half + 1) * 512],
                                           (hid_hi[:, s0 % 2, k * 128:(k + 1) * 128], hid_lo[:, s0 % 2, k * 128:(k + 1) * 128]),
                                           (w[0][:, 2 * k + half, :], w[1][:, 2 * k + half, :]),
                                           s0 == 0 and k == 0, s0 == EXP_STEPS - 1 and k == 1)
                    ins.then_inc(panel_used, 1)

                pe.wait_ge(S["hx_lo_done"], j + 1)
                def turn_pick():
                    if not first:
                        pe.wait_ge(S["x_added"], 2 * j)
                    for b in range(NB):
                        ins = pe.matmul(aux[:, 1024 + b * 128:1152 + b * 128], pick[:, b, :], ident_r[:, :], start=True, stop=True)
                    ins.then_inc(S["pick_turned"], 1)

                if first:
                    ffn_stream(EXP_STEPS, up, down, turn, after_d0=turn_pick)
                else:
                    ffn_stream(EXP_STEPS, up, down, turn, lambda: scatter(j - 1, 0), lambda: scatter(j - 1, 1), turn_pick)
                pe.wait_ge(S["pickT_done"], j + 1)
                gather(j + 1)
                turn(EXP_STEPS - 1, 0)
                down(EXP_STEPS - 1, 0)

            def scatter(j, b):
                if b == 0:
                    pe.wait_ge(S["oe_lo_done"], j + 1)
                else:
                    pe.wait_ge(S["x_added"], 2 * j + 1)
                for half in range(2):
                    for n, src in enumerate((oel, oeh)):
                        ins = pe.matmul(aux[:, 1024 + half * 512:1536 + half * 512], pickT[:, b, :],
                                        src[:, half * 512:(half + 1) * 512], start=(n == 0), stop=(n == 1))
                ins.then_inc(S["scattered"], 1)

            hxh = hT_hi[:, 0:4, :].rearrange("p k t -> p (k t)")
            hxl = hT_lo[:, 0:4, :].rearrange("p k t -> p (k t)")
            oeh = hT_hi[:, 4:8, :].rearrange("p k t -> p (k t)")
            oel = hT_lo[:, 4:8, :].rearrange("p k t -> p (k t)")
            pe.wait_ge(S["hN_lo_done"], 1)
            pe.wait_ge(S["ident_done"], 1)
            gather(0)
            expert(0, True)
            with pe.Fori(1, NE) as j:
                expert(j)
            pe.wait_ge(S["meta_done"], 1)
            m = pe.value_load(meta[0:1, 0:1], min_val=0, max_val=EXTRA)
            with pe.If(m > 0):
                with pe.Fori(NE, m + NE) as j:
                    expert(j)
            scatter(m + (NE - 1), 0)
            scatter(m + (NE - 1), 1)

        @block.vector
        def _(dve):
            own = [0]

            def link(ins):
                own[0] += 1
                ins.then_inc(v_done, 1)
                dve.wait_ge(v_done, own[0])

            def to_lo(p, slot, cols, h):
                dve.wait_ge(hi_ready, p + 1)
                nc.vector.tensor_tensor(lo_ring[:, h, 0:cols], raw(slot)[:, 0:cols], hi_ring[:, h, 0:cols].bitcast(f32),
                                        ALU.subtract).then_inc(lo_ready, 1)

            MCOLS = mixer_cols()

            def norm(n):
                dve.wait_ge(S["squared"], 2 * n + 2)
                nc.vector.tensor_scalar(small[:, 2:4], small[:, 0:2], 1.0 / D, EPS, ALU.mult, ALU.add).then_inc(S["meaned"], 1)
                dve.wait_ge(S["rooted"], n + 1)
                link(nc.vector.reciprocal(small[:, 6:8], small[:, 4:6]))
                dve.wait_ge(gain_in, 16 * (n + 1))
                for b in range(NB):
                    nc.vector.scalar_tensor_tensor(hN[:, b, :], x[:, b, :], small[:, 6 + b:7 + b], gain[:, :], ALU.mult,
                                                   ALU.mult).then_inc(S["final_done"] if n == 4 else S["normed"], 1)

            def norm_lo(n):
                for j in range(4):
                    dve.wait_ge(S["hT_hi_done"], 4 * n + j + 1)
                    o = hT_lo[:, 2 * j:2 * j + 2, :].rearrange("p k t -> p (k t)")
                    i = hT_hi[:, 2 * j:2 * j + 2, :].rearrange("p k t -> p (k t)")
                    nc.vector.tensor_tensor(o, aux[:, j * 512:(j + 1) * 512], i.bitcast(f32), ALU.subtract)\
                      .then_inc(S["hT_lo_done"], 1)

            def mixer(L):
                done = [0]

                def lo_upto(n):
                    while done[0] < min(n, MIX_PANELS):
                        i = done[0]
                        slot, _ = MSLOT[L][i]
                        p = MIX_BASE[L] + i
                        to_lo(p, slot, MCOLS[i], p % HRING)
                        done[0] += 1

                upad = ar3(A_UPAD, 4, PPAD + T)
                ypad = ar3(A_YPAD, 4, CPAD + T)
                xpad = ar3(A_XBCP, 6, SPAD + T)
                if L == 0:
                    dve.wait_ge(const_in, 16)
                    dve.wait_ge(param_in, 16)
                nc.vector.memset(upad[:, :, 0:PPAD], 0.0)
                nc.vector.memset(ypad[:, :, 0:CPAD], 0.0)
                nc.vector.memset(xpad[:, :, 0:SPAD], 0.0).then_inc(S["pads_done"], 1)
                norm(2 * L)
                norm_lo(2 * L)
                if L:
                    dve.wait_ge(param_in, 32)
                lo_upto(5)
                dve.wait_ge(*ev(L, "gt"))
                link(nc.vector.tensor_tensor(ypad[:, :, CPAD:], ar3(A_P, 4, T), ar3(A_P + 1024, 4, T), ALU.mult))
                c0 = 4 * CONV_W * L
                for t in range(CONV_W):
                    for g in range(MG):
                        i = t * MG + g
                        src = ypad[:, g, t:t + T]
                        dst = ar(A_CACC + g * T, T)
                        if t == 0:
                            ins = nc.vector.tensor_scalar(dst, src, W("conv_dw", g * CONV_W), W("conv_b", g), ALU.mult, ALU.add)
                        else:
                            dve.wait_ge(S["conved"], c0 + i - MG + 1)
                            ins = nc.vector.scalar_tensor_tensor(dst, src, W("conv_dw", g * CONV_W + t), dst, ALU.mult, ALU.add)
                        ins.then_inc(S["conved"], 1)
                        if i % 9 == 8:
                            lo_upto(done[0] + 1)
                lo_upto(19)
                dve.wait_ge(S["rotated"], L + 1)
                for o, n, rot, cs, sn in ((A_IDX, 3, 0, "cosi", "sini"), (A_QK, 5, 3 * T, "cosq", "sinq")):
                    v = ar3(o, n, T)
                    r = ar3(A_P, n, T)
                    link(nc.vector.tensor_tensor(r, aux[:, rot:rot + n * T].rearrange("p (n t) -> p n t", t=T),
                                                 C(sn).unsqueeze(1).broadcast_to([128, n, T]), ALU.mult))
                    link(nc.vector.tensor_tensor(v, v, C(cs).unsqueeze(1).broadcast_to([128, n, T]), ALU.mult))
                    ins = nc.vector.tensor_tensor(v, v, r, ALU.add)
                    if o == A_QK:
                        ins.then_inc(S["roped"], 1)
                    else:
                        link(ins)
                dve.wait_ge(S["roped"], L + 1)
                lo_upto(20)
                s1, s2 = ar3(A_P, 4, PPAD + T), ar3(A_P + 4 * (PPAD + T), 4, PPAD + T)
                link(nc.vector.memset(ar(A_P, 8 * (PPAD + T)).rearrange("p (g t) -> p g t", t=PPAD + T)[:, :, 0:PPAD], 0.0))
                dve.wait_ge(*ev(L, "pool"))
                src = upad
                where = []
                for lv, dst in enumerate((s1, s2, s1, s2)):
                    sh = 1 << lv
                    link(nc.vector.tensor_tensor(dst[:, lv:4, PPAD:], src[:, lv:4, PPAD:], src[:, lv:4, PPAD - sh:PPAD + T - sh],
                                                 ALU.add))
                    where.append(dst)
                    src = dst
                for g in range(4):
                    w = 2 << g
                    s = where[g][:, g, :]
                    u = upad[:, g, :]
                    link(nc.vector.tensor_tensor(s[:, PPAD:PPAD + 16], s[:, PPAD:PPAD + 16],
                                                 consts[:, CONSTS["invcnt"][0] + 16 * g:CONSTS["invcnt"][0] + 16 * g + 16], ALU.mult))
                    nc.vector.tensor_tensor(u[:, PPAD:PPAD + 16], s[:, PPAD:PPAD + 16], u[:, PPAD:PPAD + 16], ALU.subtract)
                    ins = nc.vector.scalar_tensor_tensor(u[:, PPAD + 16:], s[:, PPAD + 16:], 1.0 / w, u[:, PPAD + 16:],
                                                         ALU.mult, ALU.subtract)
                ins.then_inc(S["pooled"], 1)
                lo_upto(23)

                def branch_lo(i):
                    dve.wait_ge(S["branch_hi"], 4 * L + i + 1)
                    o = (i % 2) * 1024
                    nc.vector.tensor_tensor(act_lo[:, o:o + 1024], ar(A_UPAD, 1024), act_hi[:, o:o + 1024].bitcast(f32),
                                            ALU.subtract).then_inc(S["branch_lo"], 1)

                def merge(i):
                    for h in range(2):
                        name = f"br{BR_ORDER[i]}h{h}"
                        yield
                        g = pair_of(name)
                        dve.wait_ge(panel_used, used_after(L, name))
                        dve.wait_ge(*ev(L, f"g{BR_ORDER[i]}h{h}"))
                        gates = ar(A_GATES + h * 1024, 1024)
                        dst = mrg[:, h * 1024:(h + 1) * 1024]
                        if i == 0:
                            nc.vector.tensor_tensor(dst, g[:, :], gates, ALU.mult).then_inc(emptied["D"], 1)
                        else:
                            link(nc.vector.tensor_tensor(g[:, :], g[:, :], gates, ALU.mult))
                            nc.vector.tensor_tensor(dst, g[:, :], dst, ALU.add).then_inc(emptied["D"], 1)

                def score(b):
                    w = 128 * (b + 1)
                    sc = ar(A_SCORE + 128 * b, w)
                    dve.wait_ge(S["relued"], 2 * L + b + 1)
                    far = CONSTS["far"][0] + 256
                    for h in range(8):
                        ins = nc.vector.scalar_tensor_tensor(sc, ar(A_P + h * w, w), ar(A_MISC + 8 * b + h, 1),
                                                             consts[:, far - w:far] if h == 0 else sc, ALU.mult, ALU.add)
                        if h < 7:
                            link(ins)
                        else:
                            ins.then_inc(S["scored"], 1)
                            dve.wait_ge(S["scored"], 2 * L + b + 1)

                def topk(b):
                    w = 128 * (b + 1)
                    sc = ar(A_SCORE + 128 * b, w)
                    best = small[:, 16:24]
                    for _ in range(TOPK // 8):
                        link(nc.vector.max(best, sc))
                        link(nc.vector.match_replace(sc, best, sc, TAKEN))
                    mask = ar(A_MASK + 128 * b, w)
                    link(nc.vector.tensor_scalar(mask, sc, TAKEN, None, ALU.is_equal))
                    link(nc.vector.tensor_tensor(mask[:, w - 128:w], mask[:, w - 128:w], C("causal"), ALU.mult))
                    link(nc.vector.tensor_scalar(mask, mask, 1.0, -FAR, ALU.subtract, ALU.mult))

                branch_lo(0)
                score(0)
                m = merge(0)
                next(m)
                lo_upto(24)
                next(m)
                lo_upto(25)
                topk(0)
                for _ in m:
                    pass
                lo_upto(26)
                dve.wait_ge(S["ln_summed"], L + 1)
                mean = ar(A_MISC + 128, T)
                nc.vector.tensor_scalar(mean, pair_of("lnsum")[:, 0:T], 1.0 / MIX, None, ALU.mult).then_inc(emptied["D"], 1)
                dve.wait_ge(*ev(L, "lnsum"))
                cacc = ar3(A_CACC, 4, T)
                ins = nc.vector.tensor_tensor(cacc, cacc, mean.unsqueeze(1).broadcast_to([128, 4, T]), ALU.subtract)
                ins.then_inc(S["centred"], 1)
                mi = lambda o, n=16: ar(A_MISC + o, n)
                dve.wait_ge(*ev(L, "xbc1"))
                link(nc.vector.tensor_tensor(ar3(A_MISC + 16, 2, 8), ar3(A_MISC + 16, 2, 8),
                                             W("dt_bias", 0, 8).unsqueeze(1).broadcast_to([128, 2, 8]), ALU.add))
                nc.vector.scalar_tensor_tensor(mi(48), mi(16), -1.0, mi(16), ALU.mult, ALU.max).then_inc(S["dt_abs"], 1)
                lo_upto(27)
                dve.wait_ge(S["ln_varied"], L + 1)
                nc.vector.tensor_scalar(ar(A_MISC + 128, T), pair_of("lnvar")[:, 0:T], 1.0 / MIX, EPS, ALU.mult, ALU.add)\
                  .then_inc(emptied["D"], 1)
                dve.wait_ge(S["ln_rooted"], L + 1)
                link(nc.vector.reciprocal(mean, mean))
                nc.vector.tensor_tensor(cacc, cacc, mean.unsqueeze(1).broadcast_to([128, 4, T]), ALU.mult)\
                  .then_inc(S["ln_scaled"], 1)
                lo_upto(29)
                dve.wait_ge(S["ln_sig"], L + 1)
                for g in range(MG):
                    ins = nc.vector.tensor_scalar(ar(A_CACC + g * T, T), ar(A_CACC + g * T, T), W("ln_g", g), W("ln_b", g),
                                                  ALU.mult, ALU.add)
                link(ins)
                nc.vector.tensor_tensor(ar(A_UPAD, 1024), ar(A_CACC, 1024), ar(A_P, 1024), ALU.mult).then_inc(S["branch_f"], 1)
                branch_lo(1)
                score(1)
                topk(1)
                dve.wait_ge(S["dt_exp"], L + 1)
                nc.vector.tensor_scalar(mi(64), mi(48), 1.0, None, ALU.add).then_inc(S["dt_plus"], 1)
                dve.wait_ge(S["dt_plus"], L + 1)
                link(nc.vector.tensor_scalar(mi(384), mi(64), 1.0, None, ALU.subtract))
                dve.wait_ge(S["dt_ln"], L + 1)
                link(nc.vector.tensor_scalar(mi(64), mi(384), 0.0, None, ALU.is_equal))
                nc.vector.tensor_tensor(mi(80), mi(80), mi(64), ALU.add)
                link(nc.vector.tensor_tensor(mi(384), mi(384), mi(64), ALU.add))
                link(nc.vector.reciprocal(mi(384), mi(384)))
                link(nc.vector.tensor_tensor(mi(80), mi(80), mi(384), ALU.mult))
                link(nc.vector.tensor_tensor(mi(80), mi(80), mi(48), ALU.mult))
                link(nc.vector.scalar_tensor_tensor(mi(16), mi(16), 0.0, mi(80), ALU.max, ALU.add))
                dve.wait_ge(S["a_exp"], L + 1)
                nc.vector.scalar_tensor_tensor(ar3(A_MISC + 32, 2, 8), ar3(A_MISC + 16, 2, 8), -1.0,
                                               mi(112, 8).unsqueeze(1).broadcast_to([128, 2, 8]), ALU.mult, ALU.mult)\
                  .then_inc(S["dt_done"], 1)

                taps = [(t, g) for t in range(SSM_W) for g in range(6)]

                def ssm_taps(k):
                    for _ in range(k):
                        t, g = taps.pop(0)
                        src, dst = xpad[:, g, t:t + T], ar(A_XBC + g * T, T)
                        i = t * 6 + g
                        if t == 0:
                            ins = nc.vector.tensor_scalar(dst, src, W("ssm_w", g * SSM_W), W("ssm_b", g), ALU.mult, ALU.add)
                        else:
                            dve.wait_ge(S["xbc_tap"], 24 * L + i - 5)
                            ins = nc.vector.scalar_tensor_tensor(dst, src, W("ssm_w", g * SSM_W + t), dst, ALU.mult, ALU.add)
                        ins.then_inc(S["xbc_tap"], 1)

                m2 = merge(1)
                next(m2)
                for u in range(8):
                    j, b = u // 2, u % 2
                    w = 128 * (b + 1)
                    lo_upto(min(28 + u, 34) + 2)
                    dve.wait_ge(S["logits_done"], 8 * L + u + 1)
                    lg = ar3(A_CACC, 2, 256)[:, :, 0:w]
                    pr = ar3(A_CACC + 512, 2, 256)[:, :, 0:w]
                    nc.vector.scalar_tensor_tensor(lg, aux[:, 0:1024].rearrange("p (r c) -> p r c", r=2)[:, :, 0:w], 0.125,
                                                   ar(A_MASK + 128 * b, w).unsqueeze(1).broadcast_to([128, 2, w]),
                                                   ALU.mult, ALU.add).then_inc(S["logits_read"], 1)
                    dve.wait_ge(S["logits_read"], 8 * L + u + 1)
                    nc.vector.tensor_reduce(mi(96, 2), lg, AX.X, ALU.max, negate=True).then_inc(S["negmax_done"], 1)
                    ssm_taps(3)
                    dve.wait_ge(S["exped"], 8 * L + u + 1)
                    link(nc.vector.reciprocal(mi(100, 2), mi(98, 2)))
                    nc.vector.tensor_tensor(pr, pr, mi(100, 2).unsqueeze(2).broadcast_to([128, 2, w]), ALU.mult)\
                      .then_inc(S["probs_done"], 1)
                    if u == 0:
                        next(m2)
                    if u == 1:
                        for _ in m2:
                            pass
                lo_upto(36)
                branch_lo(2)
                dve.wait_ge(S["xbc_tap"], 24 * (L + 1))
                dve.wait_ge(S["xbc_sig"], L + 1)
                nc.vector.tensor_tensor(ar(A_XBC, 1536), ar(A_XBC, 1536), ar(A_P, 1536), ALU.mult).then_inc(S["xbc_done"], 1)
                lo_upto(37)
                for _ in merge(2):
                    pass
                dve.wait_ge(S["xs_turned"], L + 1)
                for b in range(NB):
                    dst = ar3(A_P + b * 512, 8, 64)
                    ins = nc.vector.tensor_tensor(dst, aux[:, b * 512:(b + 1) * 512].rearrange("p (h d) -> p h d", d=64),
                                                  mi(16 + 8 * b, 8).unsqueeze(2).broadcast_to([128, 8, 64]), ALU.mult)
                ins.then_inc(S["xd_done"], 1)
                dve.wait_ge(S["cb_done"], L + 1)
                for g in range(2):
                    o, c = A_CACC + 384 * g, 1024 + 512 * g
                    nc.vector.tensor_tensor(ar(o, 128), aux[:, c:c + 128], C("tri"), ALU.mult)
                    nc.vector.tensor_copy(ar(o + 128, 128), aux[:, c + 128:c + 256])
                    ins = nc.vector.tensor_tensor(ar(o + 256, 128), aux[:, c + 256:c + 384], C("tri"), ALU.mult)
                ins.then_inc(S["cbm_done"], 1)
                dve.wait_ge(S["acol_done"], L + 1)
                nc.vector.tensor_copy(mi(64), aux[:, 0:16]).then_inc(S["acol_read"], 1)
                dve.wait_ge(S["acol_read"], L + 1)
                dve.wait_ge(S["cbm_done"], L + 1)
                dve.wait_ge(S["z_sig"], L + 1)
                nc.vector.tensor_tensor(ar(A_Z, 1024), ar(A_Z, 1024), ar(A_UPAD, 1024), ALU.mult).then_inc(S["z_done"], 1)

                def seg(h):
                    dve.wait_ge(S["arow_done"], 2 * L + h // 4 + 1)
                    if h >= 2:
                        dve.wait_ge(S["mixm_done"], 8 * L + h - 1)
                    e, o = A_YPAD + (h % 2) * 384, (h % 4) * 256
                    nc.vector.tensor_scalar(ar(e, 256), aux[:, o:o + 256], mi(64 + h, 1), 0.0, ALU.subtract, ALU.min)
                    nc.vector.tensor_scalar(ar(e + 256, 128), aux[:, o + 128:o + 256], mi(72 + h, 1), 0.0, ALU.subtract,
                                            ALU.min).then_inc(S["arow_read"], 1)

                def mixm(h):
                    dve.wait_ge(S["decay_exp"], 8 * L + h + 1)
                    if h >= 2:
                        dve.wait_ge(S["y_done"], 8 * L + h - 1)
                    e, q = A_YPAD + (h % 2) * 384, A_P + 1024 + (h % 2) * 384
                    nc.vector.tensor_tensor(ar(q, 384), ar(e, 384), ar(A_CACC + 384 * (h // 4), 384), ALU.mult)\
                      .then_inc(S["mixm_done"], 1)

                lo_upto(38)
                seg(0)
                for h in range(8):
                    if h < 7:
                        seg(h + 1)
                    mixm(h)
                    if h % 2 == 1:
                        lo_upto(38 + h // 2 + 1)
                y = ar3(A_XBCP, 4, T)
                for g in range(MG):
                    dve.wait_ge(S["y_done"], 8 * L + 8)
                    ins = nc.vector.scalar_tensor_tensor(y[:, g, :], ar(A_XBC + g * T, T), W("dskip", g),
                                                         aux[:, 1024 + g * T:1024 + (g + 1) * T], ALU.mult, ALU.add)
                link(ins)
                dve.wait_ge(S["z_done"], L + 1)
                nc.vector.tensor_tensor(ar(A_XBCP, 1024), ar(A_XBCP, 1024), ar(A_Z, 1024), ALU.mult).then_inc(S["gated"], 1)
                lo_upto(42)
                dve.wait_ge(S["rms_summed"], L + 1)
                nc.vector.tensor_scalar(mean, pair_of("rmsum")[:, 0:T], 1.0 / MIX, EPS, ALU.mult, ALU.add)\
                  .then_inc(emptied["D"], 1)
                dve.wait_ge(S["rms_rooted"], L + 1)
                link(nc.vector.reciprocal(mean, mean))
                dve.wait_ge(S["gated"], L + 1)
                for g in range(MG):
                    ins = nc.vector.scalar_tensor_tensor(ar(A_UPAD + g * T, T), y[:, g, :], W("ssm_norm", g), mean,
                                                         ALU.mult, ALU.mult)
                ins.then_inc(S["branch_f"], 1)
                branch_lo(3)
                lo_upto(43)
                for _ in merge(3):
                    pass
                for h in range(2):
                    dve.wait_ge(S["merged_hi"], 2 * L + h + 1)
                    nc.vector.tensor_tensor(act_lo[:, h * 1024:(h + 1) * 1024], mrg[:, h * 1024:(h + 1) * 1024],
                                            act_hi[:, h * 1024:(h + 1) * 1024].bitcast(f32), ALU.subtract)\
                      .then_inc(S["merged_lo"], 1)
                lo_upto(45)
                for h in range(2):
                    if h:
                        lo_upto(46)
                    name = f"out{h}"
                    dve.wait_ge(panel_used, used_after(L, name))
                    xs = x[:, :, h * 512:(h + 1) * 512]
                    nc.vector.tensor_tensor(xs, pair_of(name)[:, :].rearrange("p (b n) -> p b n", b=NB), xs, ALU.add)\
                      .then_inc(emptied["D"], 1)

            def ffn_stream(base, mod, n, hid, hid_lo_op, start=lambda: None, after_hid0=lambda: None,
                           after_d0=lambda: None, after_a3=lambda: None, before_last=lambda: None):
                def lo(c, i):
                    to_lo(base + c + 6 * i, c % FRING, PANEL, (mod + c) % HRING)

                def step(s0, i):
                    hid(s0, i)
                    if s0 == 0:
                        after_hid0()
                    if s0 < n - 1:
                        lo(3 * s0 + 3, i)
                        hid_lo_op(s0, i)
                        lo(3 * s0 + 4, i)
                        if s0 == 0:
                            after_d0()
                        if s0 < n - 2:
                            lo(3 * s0 + 5, i)
                        if s0 == 1:
                            after_a3()
                    else:
                        lo(3 * n - 1, i)
                        before_last()
                        hid_lo_op(s0, i)

                lo(0, 0)
                lo(1, 0)
                start()
                lo(2, 0)
                step(0, 0)
                step(1, 0)
                reps = ffn_span(n)
                with dve.Fori(0, reps) as i:
                    for u in (2, 3):
                        step(u, i)
                for s in range(2 + 2 * reps, n):
                    step(s, 0)

            mixer(0)
            norm(1)
            norm_lo(1)

            def dense_hid(s0, i):
                dve.wait_ge(S["gu_silu"], s0 + 2 * i + 1)
                o = (s0 % 2) * 512
                if s0 >= 2:
                    dve.wait_ge(S["hid_hi_done"], s0 + 2 * i - 1)
                nc.vector.tensor_tensor(ar(A_HID + o, 512), pairs[s0 % 2][:, 512:1024], ar(A_SG + o, 512), ALU.mult)\
                  .then_inc(S["hid_done"], 1)

            def dense_hid_lo(s0, i):
                dve.wait_ge(S["hid_hi_done"], s0 + 2 * i + 1)
                o = (s0 % 2) * 512
                nc.vector.tensor_tensor(act_lo[:, o:o + 512], ar(A_HID + o, 512), act_hi[:, o:o + 512].bitcast(f32),
                                        ALU.subtract).then_inc(S["hid_lo_done"], 1)

            ffn_stream(DENSE_BASE, DENSE_BASE % HRING, DENSE_STEPS, dense_hid, dense_hid_lo)
            dve.wait_ge(panel_used, DENSE_BASE + DENSE_PANELS)
            for b in range(NB):
                ins = nc.vector.tensor_tensor(x[:, b, :], aux[:, b * 1024:(b + 1) * 1024], x[:, b, :], ALU.add)
            ins.then_inc(S["dense_added"], 1)

            mixer(1)
            norm(3)
            norm_lo(3)
            dve.wait_ge(S["hN_hi_done"], 1)
            nc.vector.tensor_tensor(act_lo[:, :], mrg[:, :], act_hi[:, :].bitcast(f32), ALU.subtract).then_inc(S["hN_lo_done"], 1)
            dve.wait_ge(S["router_hi"], 1)
            nc.vector.tensor_tensor(rt_lo[:, :], W("router", 0, 64), rt_hi[:, :].bitcast(f32), ALU.subtract)\
              .then_inc(S["router_split"], 1)
            R = A_SCORE
            mask, lgt, oh0, key, oh1, l2 = (ar3(R + 16 * k, 2, 8) for k in range(6))
            comb_t = ar3(R + 96, 2, SLOTS)
            pos_t = ar3(R + 96 + 2 * SLOTS, 2, SLOTS)
            p1 = ar3(R + 96 + 4 * SLOTS, 2, 8)
            sel = ar(R + 200, 8)
            cum = ar(R + 208, 8)
            over = ar(R + 216, 8)
            tmp = ar3(R + 224, 2, 8)
            rev = C("rev8").unsqueeze(1).broadcast_to([128, 2, 8])

            def first_max(src, oh, peak, at):
                link(nc.vector.tensor_reduce(peak, src, AX.X, ALU.max))
                link(nc.vector.tensor_tensor(key, src, peak.unsqueeze(2).broadcast_to([128, 2, 8]), ALU.is_equal))
                link(nc.vector.tensor_tensor(key, key, rev, ALU.mult))
                link(nc.vector.tensor_reduce(at, key, AX.X, ALU.max))
                link(nc.vector.tensor_tensor(oh, key, at.unsqueeze(2).broadcast_to([128, 2, 8]), ALU.is_equal))

            dve.wait_ge(S["routed"], 1)
            link(nc.vector.tensor_copy(lgt, aux[:, 0:16].rearrange("p (b e) -> p b e", e=8)))
            first_max(lgt, oh0, small[:, 26:28], small[:, 28:30])
            link(nc.vector.scalar_tensor_tensor(l2, oh0, FAR, lgt, ALU.mult, ALU.add))
            first_max(l2, oh1, small[:, 30:32], small[:, 28:30])
            nc.vector.tensor_tensor(small[:, 10:12], small[:, 30:32], small[:, 26:28], ALU.subtract).then_inc(S["route_read"], 1)
            nc.vector.tensor_tensor(mask, oh0, oh1, ALU.add).then_inc(S["masks_done"], 1)
            dve.wait_ge(S["route_exp"], 1)
            link(nc.vector.tensor_scalar(small[:, 32:34], small[:, 12:14], 1.0, None, ALU.add))
            link(nc.vector.reciprocal(small[:, 34:36], small[:, 32:34]))
            link(nc.vector.tensor_tensor(small[:, 36:38], small[:, 12:14], small[:, 34:36], ALU.mult))
            link(nc.vector.tensor_tensor(oh0, oh0, small[:, 34:36].unsqueeze(2).broadcast_to([128, 2, 8]), ALU.mult))
            link(nc.vector.tensor_tensor(oh1, oh1, small[:, 36:38].unsqueeze(2).broadcast_to([128, 2, 8]), ALU.mult))
            link(nc.vector.memset(ar(R + 96, 2 * SLOTS), 0.0))
            link(nc.vector.tensor_tensor(comb_t[:, :, 0:8], oh0, oh1, ALU.add))
            dve.wait_ge(S["counted"], 1)
            dve.wait_ge(S["masks_done"], 1)
            link(nc.vector.tensor_scalar(p1, aux[:, 512:528].rearrange("p (b e) -> p b e", e=8), 1.0, None, ALU.add))
            link(nc.vector.tensor_tensor(p1, p1, mask, ALU.mult))
            link(nc.vector.memset(ar(R + 96 + 2 * SLOTS, 2 * SLOTS), -1.0))
            link(nc.vector.tensor_scalar(pos_t[:, :, 0:8], p1, 1.0, None, ALU.subtract))
            link(nc.vector.tensor_scalar(over, aux[:, 528:536], 128.0, None, ALU.is_gt))
            link(nc.vector.tensor_copy(cum[:, 0:1], over[:, 0:1]))
            for e in range(1, 8):
                link(nc.vector.tensor_tensor(cum[:, e:e + 1], cum[:, e - 1:e], over[:, e:e + 1], ALU.add))
            link(nc.vector.tensor_scalar(p1, p1, 128.0, None, ALU.subtract))
            for r in range(EXTRA):
                c = NE + r
                link(nc.vector.tensor_scalar(sel, cum, float(r + 1), None, ALU.is_equal))
                link(nc.vector.tensor_tensor(sel, sel, over, ALU.mult))
                sel2 = sel.unsqueeze(1).broadcast_to([128, 2, 8])
                link(nc.vector.tensor_tensor(tmp, p1, sel2, ALU.mult))
                link(nc.vector.tensor_reduce(pos_t[:, :, c:c + 1], tmp, AX.X, ALU.add))
                link(nc.vector.tensor_scalar(pos_t[:, :, c:c + 1], pos_t[:, :, c:c + 1], 1.0, None, ALU.subtract))
                link(nc.vector.tensor_tensor(tmp, comb_t[:, :, 0:8], sel2, ALU.mult))
                link(nc.vector.tensor_reduce(comb_t[:, :, c:c + 1], tmp, AX.X, ALU.add))
                link(nc.vector.tensor_tensor(tmp[:, 0, :], sel, C("iota8"), ALU.mult))
                link(nc.vector.tensor_reduce(small[:, 41 + r:42 + r], tmp[:, 0, :], AX.X, ALU.add))
            link(nc.vector.tensor_copy(small[:, 40:41], cum[:, 7:8]))
            nc.vector.tensor_copy(meta[0:1, :], small[0:1, 40:44]).then_inc(S["meta_done"], 1)

            def make_pick(j):
                for b in range(NB):
                    ins = nc.vector.tensor_scalar(pick[:, b, :], C("iota"), arena[:, bass.ds(R + 96 + 2 * SLOTS + b * SLOTS + j, 1)],
                                                  None, ALU.is_equal)
                ins.then_inc(S["pick_done"], 1)

            def hx_lo(j):
                dve.wait_ge(S["hx_hi_done"], j + 1)
                nc.vector.tensor_tensor(hT_lo[:, 0:4, :].rearrange("p k t -> p (k t)"), aux[:, 1024:2048],
                                        hT_hi[:, 0:4, :].rearrange("p k t -> p (k t)").bitcast(f32), ALU.subtract)\
                  .then_inc(S["hx_lo_done"], 1)

            def expert(j, first=False):
                base = EXP_BASE + j * EXP_PANELS
                d0 = DENSE_STEPS + j * EXP_STEPS

                def hid(s0, i):
                    dve.wait_ge(S["gu_silu"], d0 + s0 + 2 * i + 1)
                    o = (s0 % 2) * 512
                    nc.vector.tensor_tensor(ar(A_HID + o, STEP_F), pairs[s0 % 2][:, STEP_F:512], ar(A_SG + o, STEP_F), ALU.mult)\
                      .then_inc(S["hid_done"], 1)

                def hid_lo_op(s0, i):
                    dve.wait_ge(S["hid_hi_done"], d0 + s0 + 2 * i + 1)
                    nc.vector.tensor_tensor(hid_lo[:, s0 % 2, :], pairs[s0 % 2][:, 512:512 + STEP_F],
                                            hid_hi[:, s0 % 2, :].bitcast(f32), ALU.subtract).then_inc(S["hid_lo_done"], 1)

                def next_pick():
                    dve.wait_ge(S["pickT_done"], j + 1)
                    make_pick(j + 1)

                if first:
                    ffn_stream(base, EXP_BASE % HRING, EXP_STEPS, hid, hid_lo_op, after_a3=next_pick,
                               before_last=lambda: hx_lo(j + 1))
                else:
                    ffn_stream(base, EXP_BASE % HRING, EXP_STEPS, hid, hid_lo_op, lambda: output_lo(j - 1),
                               lambda: add(j - 1, 0), lambda: add(j - 1, 1), next_pick, lambda: hx_lo(j + 1))

            def output_lo(j):
                dve.wait_ge(S["oe_hi_done"], j + 1)
                nc.vector.tensor_tensor(hT_lo[:, 4:8, :].rearrange("p k t -> p (k t)"), aux[:, 0:1024],
                                        hT_hi[:, 4:8, :].rearrange("p k t -> p (k t)").bitcast(f32), ALU.subtract)\
                  .then_inc(S["oe_lo_done"], 1)

            def add(j, b):
                dve.wait_ge(S["scattered"], 2 * j + b + 1)
                nc.vector.scalar_tensor_tensor(x[:, b, :], aux[:, 1024:2048], arena[:, bass.ds(R + 96 + b * SLOTS + j, 1)],
                                               x[:, b, :], ALU.mult, ALU.add).then_inc(S["x_added"], 1)
                if b:
                    dve.wait_ge(S["x_added"], 2 * j + 2)

            make_pick(0)
            hx_lo(0)
            expert(0, True)
            with dve.Fori(1, NE) as j:
                expert(j)
            dve.wait_ge(S["meta_done"], 1)
            m = dve.value_load(meta[0:1, 0:1], min_val=0, max_val=EXTRA)
            with dve.If(m > 0):
                with dve.Fori(NE, m + NE) as j:
                    expert(j)
            output_lo(m + (NE - 1))
            add(m + (NE - 1), 0)
            add(m + (NE - 1), 1)
            nc.vector.tensor_copy(small[:, 24:25], small[:, 0:1]).then_inc(S["extra_done"], 1)
            norm(4)


def mixer_cols():
    width = {"kiwi": 40, "xbc1": 264}
    return [4 * width.get(n, 512) for n, k, _ in CHUNKS for _ in range(k)]


def constants():
    c = np.zeros((128, NCONST), np.float32)
    i = np.arange(128)

    def put(name, v):
        c[:, CONSTS[name][0]:CONSTS[name][0] + CONSTS[name][1]] = v

    put("ident", np.eye(128))
    put("tri", i[:, None] <= i[None, :])
    put("ones", 1.0)
    put("strict", i[:, None] < i[None, :])
    put("causal", i[None, :] <= i[:, None])
    put("far", np.concatenate([np.zeros((128, 128)), np.where(i[None, :] <= i[:, None], 0.0, FAR)], 1))
    put("swap", i[:, None] == (i[None, :] + 64) % 128)
    put("iota", i[None, :])
    put("rev8", np.arange(8, 0, -1)[None, :])
    put("iota8", np.arange(8)[None, :])
    put("invcnt", np.concatenate([1.0 / np.minimum(np.arange(16) + 1, 2 << g) for g in range(4)]).astype(np.float32)[None, :])
    for dim, tag in ((64, "q"), (32, "i")):
        half = dim // 8
        rot = np.zeros((128, 128), np.float32)
        inv = np.power(np.float32(500000.0), -np.arange(half, dtype=np.float32) * np.float32(1.0 / half)).astype(np.float32)
        ang = (np.arange(T, dtype=np.float32)[None, :] * inv[:, None]).astype(np.float32)
        cos, sin = np.ones((128, T), np.float32), np.zeros((128, T), np.float32)
        for a in range(0, 128, dim):
            for k in range(half):
                rot[a + half + k, a + k] = -1.0
                rot[a + k, a + half + k] = 1.0
            for o in (0, half):
                cos[a + o:a + o + half] = np.cos(ang)
                sin[a + o:a + o + half] = np.sin(ang)
        put("rot" + tag, rot)
        put("cos" + tag, cos)
        put("sin" + tag, sin)
    return c


def kernel(**inputs):
    import concourse.bacc as bacc
    from concourse.bass_utils import run_bass_kernel_spmd as run

    a = {k: np.ascontiguousarray(v) for k, v in inputs.items()}

    def cols(v):
        return v.reshape(-1, 128).T

    params = []
    for L in range(2):
        params.append(np.concatenate([
            a["pool_w"][L].transpose(1, 0, 2).reshape(128, 512), cols(a["pool_scale"][L]),
            a["conv_dw"][L].reshape(CONV_W, 4, 128).transpose(2, 1, 0).reshape(128, 4 * CONV_W), cols(a["conv_b"][L]),
            cols(a["conv_ln_g"][L]), cols(a["conv_ln_b"][L]),
            a["ssm_conv_w"][L].reshape(SSM_W, 6, 128).transpose(2, 1, 0).reshape(128, 24), cols(a["ssm_conv_b"][L]),
            cols(np.repeat(a["ssm_d"][L], 64)), cols(a["ssm_norm"][L]),
            np.broadcast_to(a["ssm_dt_bias"][L][None], (128, 8)), np.broadcast_to(a["ssm_a_log"][L][None], (128, 8)),
            a["moe_router"][0].reshape(8, 128, 8).transpose(1, 0, 2).reshape(128, 64)], axis=1))
    gains = np.stack([a["norm_mix"][0], a["norm_ffn"][0], a["norm_mix"][1], a["norm_ffn"][1], a["final_norm"]])
    arrays = {"in_x": a["x"][0], "in_gains": gains, "in_consts": constants(), "in_params": np.ascontiguousarray(np.stack(params)),
              "in_w_in": a["w_in"], "in_w_br": a["w_br"], "in_w_out": a["w_out"],
              "in_fg": a["ffn_w_gate"][0], "in_fu": a["ffn_w_up"][0], "in_fd": a["ffn_w_down"][0],
              "in_mg": a["moe_w_gate"][0], "in_mu": a["moe_w_up"][0], "in_md": a["moe_w_down"][0]}
    nc = bacc.Bacc("TRN2", target_bir_lowering=False, num_devices=1)
    aps = [nc.dram_tensor(k, v.shape, mybir.dt.float32, kind="ExternalInput").ap() for k, v in arrays.items()]
    out = nc.dram_tensor("out_y", (T, D), mybir.dt.float32, kind="ExternalOutput").ap()
    build(nc, *aps, out)
    r = run(nc, [arrays], core_ids=[0])
    return r.results[0]["out_y"].reshape(1, T, D)
```

```python
import numpy as np
import concourse.bass as bass
from concourse import mybir
from contextlib import ExitStack

D = 1024
T = 256
NB = T // 128
KT = D // 128
MIX = 512
MG = MIX // 128
F_DENSE = 2816
F_EXP = 3584
NE = 8
CONV_W = 31
CPAD = CONV_W - 1
SSM_W = 4
SPAD = SSM_W - 1
PPAD = 16
TOPK = T // 4
HEADS = 8
EPS = 1e-6
FAR = -3.0e38
TAKEN = -3.4e38
SLAB = 512
PANEL = 4 * SLAB
STEP_F = 256
DENSE_STEPS = F_DENSE // STEP_F
EXP_STEPS = F_EXP // STEP_F
MIX_PANELS = 46
UNIT_PANEL = 25
HEAD_PANEL = 34
DENSE_PANELS = 3 * DENSE_STEPS
EXP_PANELS = 3 * EXP_STEPS
HRING = 3
MRING = 3
FRING = 6
EXTRA = 3
SLOTS = NE + EXTRA + 1

C_POOL, C_Q, C_KVQI, C_KIWI = 0, 512, 1024, 1536
C_A, C_GT, C_Z, C_XBC0, C_XBC1, C_GATE = 1576, 2088, 2600, 3112, 3624, 3888

CHUNKS = [("a", 2, "A"), ("gt", 2, "A"), ("kiwi", 2, "A"), ("kvqi", 2, "A"), ("q", 2, "A"), ("pool", 2, "A"),
          ("xbc0", 2, "A"), ("xbc1", 2, "A"), ("lnsum", 0, "D"), ("z", 2, "A"), ("lnvar", 0, "D"),
          ("g2h0", 2, "A"), ("g2h1", 2, "A"), ("pooly", 0, "A"), ("br2h0", 1, "D"), ("br2h1", 1, "D"),
          ("g0h0", 2, "A"), ("g0h1", 2, "A"), ("br0h0", 1, "D"), ("br0h1", 1, "D"),
          ("g1h0", 2, "A"), ("g1h1", 2, "A"), ("br1h0", 1, "D"), ("br1h1", 1, "D"),
          ("g3h0", 2, "A"), ("g3h1", 2, "A"), ("rmsum", 0, "D"), ("br3h0", 1, "D"), ("br3h1", 1, "D"),
          ("out0", 2, "D"), ("out1", 2, "D")]
BR_ORDER = [2, 0, 1, 3]
NCH = len(CHUNKS)
CH_INDEX = {c[0]: i for i, c in enumerate(CHUNKS)}
CH_PANEL = {}
_p = 0
for _n, _k, _e in CHUNKS:
    CH_PANEL[_n] = _p
    _p += _k
assert _p == MIX_PANELS
N_EVA = sum(1 for c in CHUNKS if c[2] == "A")
N_EVD = NCH - N_EVA

CONSTS = {}
_c = 0
for _n, _w in (("ident", 128), ("tri", 128), ("ones", 128), ("strict", 128), ("rotq", 128), ("roti", 128),
               ("swap", 128), ("cosq", 256), ("sinq", 256), ("cosi", 256), ("sini", 256), ("iota", 128),
               ("invcnt", 64), ("far", 256), ("causal", 128), ("rev8", 8), ("iota8", 8)):
    CONSTS[_n] = (_c, _w)
    _c += _w
NCONST = _c
PARAMS = {}
_c = 0
for _n, _w in (("pool_w", 512), ("pool_scale", 4), ("conv_dw", 4 * CONV_W), ("conv_b", 4), ("ln_g", 4), ("ln_b", 4),
               ("ssm_w", 24), ("ssm_b", 6), ("dskip", 4), ("ssm_norm", 4), ("dt_bias", 8), ("a_log", 8), ("router", 64)):
    PARAMS[_n] = (_c, _w)
    _c += _w
NPARAM = _c

A_P, A_YPAD, A_CACC, A_QK, A_IDX = 0, 2176, 3320, 4344, 5624
A_KI, A_V, A_UPAD, A_XBCP, A_XBC, A_Z, A_GATES = 6392, 6904, 7160, 8248, 9802, 11338, 12362
A_SCORE, A_MASK, A_MISC = 14410, 14794, 15178
A_END = 15178 + 400
A_RAW = 0
A_SG, A_HID = 3 * PANEL, 3 * PANEL + 1024


def build(nc, x_d, gains_d, consts_d, params_d, w_in, w_br, w_out, fg, fu, fd, mg, mu, md, out_d):
    f32, f32r, i32 = mybir.dt.float32, mybir.dt.float32r, mybir.dt.int32
    ALU, ACT, AX = mybir.AluOpType, mybir.ActivationFunctionType, mybir.AxisListType
    ctx = ExitStack()
    with ctx:
        def sb(name, shape, dt=f32):
            return ctx.enter_context(nc.sbuf_tensor(name, shape, dt))

        def sem(name):
            return ctx.enter_context(nc.semaphore(name))

        raw_ring = sb("raw_ring", [128, MRING * PANEL])
        hi_ring = sb("hi_ring", [128, HRING, PANEL], f32r)
        lo_ring = sb("lo_ring", [128, HRING, PANEL], f32r)
        x = sb("x", [128, NB, D])
        hT_hi = sb("hT_hi", [128, KT, T], f32r)
        hT_lo = sb("hT_lo", [128, KT, T], f32r)
        act_hi = sb("act_hi", [128, 2048], f32r)
        act_lo = sb("act_lo", [128, 2048], f32r)
        hid_hi = sb("hid_hi", [128, 2, STEP_F], f32r)
        hid_lo = sb("hid_lo", [128, 2, STEP_F], f32r)
        pick = sb("pick", [128, NB, 128], f32r)
        pickT = sb("pickT", [128, NB, 128], f32r)
        ident_r = sb("ident_r", [128, 128], f32r)
        rt_hi = sb("rt_hi", [128, 64], f32r)
        rt_lo = sb("rt_lo", [128, 64], f32r)
        consts = sb("consts", [128, NCONST])
        params = sb("params", [128, NPARAM])
        gain = sb("gain", [128, D])
        mrg = sb("mrg", [128, 2 * D])
        arena = sb("arena", [128, A_END])
        small = sb("small", [128, 64])
        meta = sb("meta", [1, 4], i32)
        pairs = [ctx.enter_context(nc.psum_tensor(f"pair{i}", [128, 1024], f32)) for i in range(2)]
        aux = ctx.enter_context(nc.psum_tensor("aux", [128, 2048], f32))

        def C(n):
            return consts[:, CONSTS[n][0]:CONSTS[n][0] + CONSTS[n][1]]

        def W(n, i=0, k=1):
            o = PARAMS[n][0]
            return params[:, o + i:o + i + k]

        def ar(o, n):
            return arena[:, o:o + n]

        def ar3(o, a, b):
            return arena[:, o:o + a * b].rearrange("p (a b) -> p a b", b=b)

        def raw(slot):
            if slot < MRING:
                return raw_ring[:, slot * PANEL:(slot + 1) * PANEL]
            return arena[:, A_RAW + (slot - MRING) * PANEL:A_RAW + (slot - MRING + 1) * PANEL]

        hN = mrg[:, :].rearrange("p (b d) -> p b d", b=NB)
        merged = mrg[:, :].rearrange("p (g t) -> p g t", t=T)

        raw_in = [sem(f"raw_in{i}") for i in range(FRING)]
        x_in, ident_in, const_in, param_in, gain_in, stored = sem("x_in"), sem("ident_in"), sem("const_in"), sem("param_in"), sem("gain_in"), sem("stored")
        hi_ready, lo_ready, panel_used = sem("hi_ready"), sem("lo_ready"), sem("panel_used")
        emptied = {"A": sem("emptied_by_act"), "D": sem("emptied_by_dve")}
        v_done, a_done = sem("v_done"), sem("a_done")
        names = ["squared", "meaned", "rooted", "normed", "turned", "hT_hi_done", "hT_lo_done", "ki_turned",
                 "ki_copied", "rotated", "roped", "k_swapped", "k_copied", "indexed", "relued", "scored", "conved",
                 "ln_summed", "centred", "ln_squared", "ln_varied", "ln_rooted", "ln_scaled", "ln_sig", "pooled",
                 "pool_mixed", "branch_f", "branch_hi", "branch_lo", "merged_hi", "merged_lo", "logits_done",
                 "logits_read", "negmax_done", "exped", "probs_done", "probs_turned", "probs_copied", "attended",
                 "att_copied", "xbc_sig", "xbc_done", "dt_abs", "dt_exp", "dt_plus", "dt_ln", "dt_done", "a_exp",
                 "xs_turned", "xd_done", "cb_done", "cbm_done", "acol_done", "acol_read", "arow_done", "arow_read",
                 "decay_exp", "mixm_done", "y_done", "z_sig", "gated", "rms_squared", "rms_summed", "rms_rooted",
                 "gu_silu", "hid_done", "hid_hi_done", "hid_lo_done", "hid_turned", "router_split", "routed_T",
                 "routed_copied", "routed", "route_read", "route_exp", "masks_done", "counted", "pick_done",
                 "pick_turned", "pickT_done", "gathered", "hx_hi_done", "hx_lo_done", "oe_hi_done", "oe_lo_done",
                 "scattered", "x_added", "meta_done", "hN_hi_done", "hN_lo_done", "final_done", "ident_done",
                 "pads_done", "extra_done", "router_hi", "xbc_tap", "one_set", "z_done", "dense_added"]
        S = {n: sem(n) for n in names}

        block = ctx.enter_context(nc.Block())

        MIX_BASE = [0, MIX_PANELS + DENSE_PANELS]
        DENSE_BASE = MIX_PANELS
        EXP_BASE = MIX_BASE[1] + MIX_PANELS

        uses = [0] * FRING
        MSLOT = [[], []]
        DENSE_USE0, EXP_USE0 = None, None
        for L in range(2):
            for i in range(MIX_PANELS):
                s = i % MRING
                MSLOT[L].append((s, uses[s]))
                uses[s] += 1
            if L == 0:
                DENSE_USE0 = list(uses)
                for i in range(DENSE_PANELS):
                    uses[i % FRING] += 1
            else:
                EXP_USE0 = list(uses)

        def ev(L, name):
            who = CHUNKS[CH_INDEX[name]][2]
            n = sum(1 for c in CHUNKS[:CH_INDEX[name] + 1] if c[2] == who)
            return emptied[who], L * (N_EVA if who == "A" else N_EVD) + n

        def pair_of(name):
            return pairs[CH_INDEX[name] % 2]

        def used_after(L, name):
            return MIX_BASE[L] + CH_PANEL[name] + CHUNKS[CH_INDEX[name]][1]

        def ffn_span(n):
            return (n - 4) // 2

        @block.sync
        def _(sp):
            sp.dma_start(x[:, :, :], x_d.rearrange("(b p) d -> p b d", p=128)).then_inc(x_in, 16)
            last = {}

            def halves(slot, width, src):
                for h in range(2):
                    sp.dma_start(raw(slot)[:, 2 * h * width:2 * (h + 1) * width].rearrange("p (k n) -> p k n", n=width),
                                 src[:, 2 * h:2 * h + 2, :]).then_inc(raw_in[slot], 16)

            def mixer(L):
                i = 0

                def panel(width, src):
                    nonlocal i
                    slot, _ = MSLOT[L][i]
                    p = MIX_BASE[L] + i
                    if slot in last:
                        sp.wait_ge(lo_ready, last[slot] + 1)
                    halves(slot, width, src)
                    last[slot] = p
                    i += 1

                def chunk_in(c0, width):
                    for kh in range(2):
                        panel(width, w_in[L, kh * 512:(kh + 1) * 512, c0:c0 + width].rearrange("(k p) n -> p k n", p=128))

                for c0, width in ((C_A, 512), (C_GT, 512), (C_KIWI, 40), (C_KVQI, 512), (C_Q, 512), (C_POOL, 512),
                                  (C_XBC0, 512), (C_XBC1, 264), (C_Z, 512)):
                    chunk_in(c0, width)

                def gates(n):
                    for h in range(2):
                        chunk_in(C_GATE + n * D + h * 512, 512)

                def branch(n):
                    for h in range(2):
                        panel(512, w_br[L, n, :, h * 512:(h + 1) * 512].rearrange("(k p) n -> p k n", p=128))

                gates(2)
                branch(2)
                gates(0)
                branch(0)
                gates(1)
                branch(1)
                gates(3)
                branch(3)
                for h in range(2):
                    for kh in range(2):
                        panel(512, w_out[L, kh * 512:(kh + 1) * 512, h * 512:(h + 1) * 512].rearrange("(k p) n -> p k n", p=128))

            def ffn_panel(p, slot, dst_src):
                sp.wait_ge(lo_ready, p - (FRING - 1))
                for dst, src in dst_src:
                    sp.dma_start(dst, src).then_inc(raw_in[slot], 16)

            def ffn_stream(base, n, wg, wu, wd):
                def up(s0, i):
                    for kh in range(2):
                        c = (3 * s0 - 1 if s0 else 0) + kh
                        slot = c % FRING
                        v = raw(slot).rearrange("p (k n) -> p k n", n=512)
                        s = s0 + 2 * i
                        ffn_panel(base + c + 6 * i, slot,
                                  ((v[:, :, 0:STEP_F], wg(kh, s)), (v[:, :, STEP_F:512], wu(kh, s))))

                def down(s0, i):
                    c = 3 * n - 1 if s0 == n - 1 else 3 * s0 + 4
                    slot = c % FRING
                    v = raw(slot).rearrange("p (k n) -> p k n", n=D)
                    src = wd(s0 + 2 * i)
                    ffn_panel(base + c + 6 * i, slot, ((v[:, 0:1, :], src[:, 0:1, :]), (v[:, 1:2, :], src[:, 1:2, :])))

                up(0, 0)
                up(1, 0)
                down(0, 0)
                reps = ffn_span(n)
                with sp.Fori(0, reps) as i:
                    for u in (2, 3):
                        up(u, i)
                        down(u - 1, i)
                for s in range(2 + 2 * reps, n):
                    up(s, 0)
                    down(s - 1, 0)
                down(n - 1, 0)

            mixer(0)
            sp.wait_ge(lo_ready, DENSE_BASE)
            sp.wait_ge(*ev(0, "br3h1"))
            ffn_stream(DENSE_BASE, DENSE_STEPS,
                       lambda kh, s: fg[kh * 512:(kh + 1) * 512, bass.ds(s * STEP_F, STEP_F)].rearrange("(k p) n -> p k n", p=128),
                       lambda kh, s: fu[kh * 512:(kh + 1) * 512, bass.ds(s * STEP_F, STEP_F)].rearrange("(k p) n -> p k n", p=128),
                       lambda s: fd[bass.ds(s * STEP_F, STEP_F), :].rearrange("(k p) n -> p k n", p=128))
            for i in range(DENSE_PANELS):
                last[i % FRING] = DENSE_BASE + i
            mixer(1)
            sp.wait_ge(lo_ready, EXP_BASE)
            sp.wait_ge(*ev(1, "br3h1"))

            def expert(j, e):
                def rows(w, kh, s):
                    return w[bass.ds(e, 1), kh * 512:(kh + 1) * 512, bass.ds(s * STEP_F, STEP_F)].rearrange("a (k p) n -> p (a k) n", p=128)
                ffn_stream(EXP_BASE + j * EXP_PANELS, EXP_STEPS,
                           lambda kh, s: rows(mg, kh, s), lambda kh, s: rows(mu, kh, s),
                           lambda s: md[bass.ds(e, 1), bass.ds(s * STEP_F, STEP_F), :].rearrange("a (k p) n -> p (a k) n", p=128))

            with sp.Fori(0, NE) as j:
                expert(j, j)
            sp.wait_ge(S["meta_done"], 1)
            m = sp.value_load(meta[0:1, 0:1], min_val=0, max_val=EXTRA)
            with sp.If(m > 0):
                with sp.Fori(NE, m + NE) as j:
                    expert(j, sp.value_load(meta[0:1, bass.ds(j - (NE - 1), 1)], min_val=0, max_val=NE - 1))

            for b in range(NB):
                sp.wait_ge(S["final_done"], b + 1)
                sp.dma_start(out_d[b * 128:(b + 1) * 128, :], hN[:, b, :]).then_inc(stored, 16)
            sp.wait_ge(stored, 16 * NB)

        @block.gpsimd
        def _(pool):
            pool.dma_start(consts[:, 0:128], consts_d[:, 0:128]).then_inc(ident_in, 16)
            for n in range(5):
                if n:
                    pool.wait_ge(S["normed"], 2 * n)
                pool.dma_start(gain[:, :], gains_d[n:n + 1, :].broadcast_to([128, D])).then_inc(gain_in, 16)
                if n == 0:
                    pool.dma_start(params[:, :], params_d[0, :, :]).then_inc(param_in, 16)
                    pool.dma_start(consts[:, 128:], consts_d[:, 128:]).then_inc(const_in, 16)
                if n == 1:
                    pool.wait_ge(*ev(0, "br3h1"))
                    pool.dma_start(params[:, :], params_d[1, :, :]).then_inc(param_in, 16)

        @block.scalar
        def _(act):
            own = [0]

            def link(ins):
                own[0] += 1
                ins.then_inc(a_done, 1)
                act.wait_ge(a_done, own[0])

            def to_hi(p, slot, use, cols, h=None):
                act.wait_ge(raw_in[slot], 32 * (use + 1))
                if not (isinstance(p, int) and p < HRING):
                    act.wait_ge(panel_used, p - (HRING - 1))
                nc.scalar.activation(hi_ring[:, h, 0:cols], raw(slot)[:, 0:cols], ACT.Copy).then_inc(hi_ready, 1)

            MCOLS = mixer_cols()

            def warm_sqrt():
                nc.scalar.activation(small[:, 45:46], small[:, 44:45], ACT.Sqrt)

            def norm(n):
                if n == 0:
                    act.wait_ge(S["one_set"], 1)
                warm_sqrt()
                for b in range(NB):
                    if n == 0 and b == 0:
                        act.wait_ge(x_in, 16)
                    if n and b == 0:
                        act.wait_ge(*{1: ev(0, "out1"), 2: (S["dense_added"], 1), 3: ev(1, "out1")}[n])
                    nc.scalar.activation(hN[:, b, :], x[:, b, :], ACT.Square,
                                         accum_out=small[:, b:b + 1]).then_inc(S["squared"], 1)
                act.wait_ge(S["meaned"], n + 1)
                nc.scalar.activation(small[:, 4:6], small[:, 2:4], ACT.Sqrt).then_inc(S["rooted"], 1)

            def norm_hi(n):
                for j in range(4):
                    act.wait_ge(S["turned"], 4 * n + j + 1)
                    nc.scalar.activation(hT_hi[:, 2 * j:2 * j + 2, :].rearrange("p k t -> p (k t)"),
                                         aux[:, j * 512:(j + 1) * 512], ACT.Copy).then_inc(S["hT_hi_done"], 1)

            def mixer(L):
                done = [0]

                def hi_upto(n):
                    while done[0] < min(n, MIX_PANELS):
                        i = done[0]
                        slot, use = MSLOT[L][i]
                        p = MIX_BASE[L] + i
                        to_hi(p, slot, use, MCOLS[i], p % HRING)
                        done[0] += 1

                def after(name):
                    hi_upto(CH_PANEL[name] + CHUNKS[CH_INDEX[name]][1] + 2)
                    act.wait_ge(panel_used, used_after(L, name))

                def evac(out, in_, func=ACT.Copy, scale=1.0, last=False):
                    ins = nc.scalar.activation(out, in_, func, scale=scale)
                    if last:
                        ins.then_inc(emptied["A"], 1)

                if L:
                    hi_upto(2)
                    act.wait_ge(S["pads_done"], L + 1)
                norm(2 * L)
                hi_upto(2 + L)
                norm_hi(2 * L)
                hi_upto(3)
                if L == 0:
                    act.wait_ge(ident_in, 16)
                    nc.scalar.activation(ident_r[:, :], C("ident"), ACT.Copy).then_inc(S["ident_done"], 1)
                after("a")
                evac(ar(A_P, 1024), pair_of("a")[:, :], last=True)
                after("gt")
                evac(ar(A_P + 1024, 1024), pair_of("gt")[:, :], ACT.Sigmoid, last=True)
                after("kiwi")
                g = pair_of("kiwi")
                for b in range(NB):
                    evac(ar3(A_KI + b * 128, 4, 32), g[:, b * 40:b * 40 + 32].unsqueeze(1).broadcast_to([128, 4, 32]))
                    evac(ar(A_MISC + b * 8, 8), g[:, b * 40 + 32:b * 40 + 40], last=(b == NB - 1))
                after("kvqi")
                g = pair_of("kvqi")
                evac(ar(A_QK + 1024, 256), g[:, 0:256])
                evac(ar(A_V, 256), g[:, 256:512])
                evac(ar(A_IDX, 512), g[:, 512:1024], last=True)
                after("q")
                evac(ar(A_QK, 1024), pair_of("q")[:, :], last=True)
                after("pool")
                evac(ar3(A_UPAD, 4, PPAD + T)[:, :, PPAD:], pair_of("pool")[:, :].rearrange("p (g t) -> p g t", t=T), last=True)
                act.wait_ge(S["ki_turned"], L + 1)
                nc.scalar.activation(ar(A_IDX + 512, 256), aux[:, 0:256], ACT.Copy).then_inc(S["ki_copied"], 1)
                after("xbc0")
                evac(ar3(A_XBCP, 6, SPAD + T)[:, 0:4, SPAD:], pair_of("xbc0")[:, :].rearrange("p (g t) -> p g t", t=T), last=True)
                after("xbc1")
                g = pair_of("xbc1")
                evac(ar3(A_XBCP, 6, SPAD + T)[:, 4:6, SPAD:], g[:, 0:512].rearrange("p (g t) -> p g t", t=T))
                evac(ar(A_MISC + 16, 16), g[:, 512:528], last=True)

                def gate(name, before=None):
                    after(name)
                    if before:
                        act.wait_ge(*ev(L, before))
                    h = int(name[3])
                    evac(ar(A_GATES + h * 1024, 1024), pair_of(name)[:, :], ACT.Sigmoid, last=True)

                def branch_hi(i, src=A_UPAD):
                    nc.scalar.activation(act_hi[:, (i % 2) * 1024:(i % 2 + 1) * 1024], ar(src, 1024), ACT.Copy)\
                       .then_inc(S["branch_hi"], 1)

                def relu(b):
                    act.wait_ge(S["indexed"], 2 * L + b + 1)
                    if b == 0:
                        act.wait_ge(S["pooled"], L + 1)
                    else:
                        act.wait_ge(S["scored"], 2 * L + b)
                    w = 128 * (b + 1)
                    nc.scalar.activation(ar3(A_P, 8, w).rearrange("p (h j) w -> p j h w", j=4),
                                         aux[:, :].rearrange("p (j c) -> p j c", j=4)[:, :, 0:2 * w]
                                         .rearrange("p j (h w) -> p j h w", w=w), ACT.Relu).then_inc(S["relued"], 1)

                act.wait_ge(S["centred"], L + 1)
                nc.scalar.activation(ar(A_YPAD, 1024), ar(A_CACC, 1024), ACT.Square).then_inc(S["ln_squared"], 1)
                act.wait_ge(S["dt_abs"], L + 1)
                nc.scalar.activation(ar(A_MISC + 48, 16), ar(A_MISC + 48, 16), ACT.Exp, scale=-1.0).then_inc(S["dt_exp"], 1)
                nc.scalar.activation(ar(A_MISC + 112, 8), W("a_log", 0, 8), ACT.Exp).then_inc(S["a_exp"], 1)
                act.wait_ge(S["dt_plus"], L + 1)
                nc.scalar.activation(ar(A_MISC + 80, 16), ar(A_MISC + 64, 16), ACT.Ln).then_inc(S["dt_ln"], 1)
                after("z")
                evac(ar(A_Z, 1024), pair_of("z")[:, :], last=True)
                act.wait_ge(*ev(L, "lnvar"))
                nc.scalar.activation(ar(A_MISC + 128, T), ar(A_MISC + 128, T), ACT.Sqrt).then_inc(S["ln_rooted"], 1)
                hi_upto(CH_PANEL["g2h1"] + 1)
                act.wait_ge(S["ln_scaled"], L + 1)
                for g in range(MG):
                    ins = nc.scalar.activation(ar(A_YPAD + g * T, T), ar(A_CACC + g * T, T), ACT.Sigmoid,
                                               scale=W("ln_g", g), bias=W("ln_b", g))
                ins.then_inc(S["ln_sig"], 1)
                gate("g2h0")
                hi_upto(CH_PANEL["br2h1"])
                act.wait_ge(S["branch_f"], 2 * L + 1)
                branch_hi(0, A_CACC)
                act.wait_ge(S["k_swapped"], L + 1)
                nc.scalar.activation(ar(A_KI, 256), aux[:, 0:256], ACT.Copy).then_inc(S["k_copied"], 1)
                gate("g2h1")
                relu(0)
                act.wait_ge(S["pool_mixed"], L + 1)
                for g in range(MG):
                    ins = nc.scalar.activation(ar(A_UPAD + g * T, T), pair_of("pooly")[:, g * T:(g + 1) * T], ACT.Copy,
                                               scale=W("pool_scale", g))
                ins.then_inc(emptied["A"], 1)
                act.wait_ge(*ev(L, "pooly"))
                branch_hi(1)
                hi_upto(25)
                relu(1)
                hi_upto(26)

                def exps(u):
                    j, b = u % 4, u // 4
                    w = 128 * (b + 1)
                    act.wait_ge(S["negmax_done"], 8 * L + u + 1)
                    for r in range(2):
                        ins = nc.scalar.activation(ar(A_CACC + 512 + r * 256, w), ar(A_CACC + r * 256, w), ACT.Exp,
                                                   bias=ar(A_MISC + 96 + r, 1), accum_out=ar(A_MISC + 98 + r, 1))
                    ins.then_inc(S["exped"], 1)

                def probs_out(u):
                    j, b = u % 4, u // 4
                    act.wait_ge(S["probs_turned"], 8 * L + u + 1)
                    n = 2 * (b + 1) * 128
                    nc.scalar.activation(ar(A_YPAD, n), aux[:, 1024:1024 + n], ACT.Copy).then_inc(S["probs_copied"], 1)

                def att_out(u):
                    j, b = u % 4, u // 4
                    act.wait_ge(S["attended"], 8 * L + u + 1)
                    nc.scalar.activation(ar(A_UPAD + j * T + b * 128, 128), aux[:, 1536 + j * 128:1664 + j * 128], ACT.Copy)\
                       .then_inc(S["att_copied"], 1)

                act.wait_ge(S["branch_lo"], 4 * L + 2)
                for u in range(8):
                    hi_upto(UNIT_PANEL + u + 2)
                    exps(u)
                    hi_upto(UNIT_PANEL + u + 3)
                    if u:
                        att_out(u - 1)
                    probs_out(u)
                    if u == 0:
                        gate("g0h0", "br2h0")
                    if u == 2:
                        gate("g0h1", "br2h1")
                    if u == 6:
                        gate("g1h0", "br0h0")
                        act.wait_ge(S["xbc_tap"], 24 * (L + 1))
                        nc.scalar.activation(ar(A_P, 1536), ar(A_XBC, 1536), ACT.Sigmoid).then_inc(S["xbc_sig"], 1)
                        nc.scalar.activation(ar(A_XBCP, 1024), ar(A_Z, 1024), ACT.Sigmoid).then_inc(S["z_sig"], 1)
                att_out(7)
                act.wait_ge(S["att_copied"], 8 * (L + 1))
                branch_hi(2)
                gate("g1h1", "br0h1")

                def decay(h):
                    act.wait_ge(S["arow_read"], 8 * L + h + 1)
                    e = A_YPAD + (h % 2) * 384
                    nc.scalar.activation(ar(e, 384), ar(e, 384), ACT.Exp).then_inc(S["decay_exp"], 1)

                for h in range(8):
                    if h % 2 == 0:
                        hi_upto(HEAD_PANEL + h // 2 + 3)
                    decay(h)
                gate("g3h0", "br1h0")
                hi_upto(CH_PANEL["br3h0"] + 1)
                act.wait_ge(S["gated"], L + 1)
                nc.scalar.activation(ar(A_P, 1024), ar(A_XBCP, 1024), ACT.Square).then_inc(S["rms_squared"], 1)
                act.wait_ge(*ev(L, "rmsum"))
                nc.scalar.activation(ar(A_MISC + 128, T), ar(A_MISC + 128, T), ACT.Sqrt).then_inc(S["rms_rooted"], 1)
                act.wait_ge(S["branch_f"], 2 * L + 2)
                branch_hi(3)
                gate("g3h1", "br1h1")
                hi_upto(CH_PANEL["out0"] + 1)
                for h in range(2):
                    hi_upto(CH_PANEL["out0"] + 2 + h)
                    act.wait_ge(*ev(L, f"br3h{h}"))
                    act.wait_ge(panel_used, used_after(L, f"br{BR_ORDER[2 + h]}h1"))
                    nc.scalar.activation(act_hi[:, h * 1024:(h + 1) * 1024], mrg[:, h * 1024:(h + 1) * 1024], ACT.Copy)\
                       .then_inc(S["merged_hi"], 1)
                hi_upto(MIX_PANELS)

            def ffn_stream(base, use0, n, silu, hid_hi_op, ahead=False, start=lambda: None, middle=lambda: None, last=lambda: None):
                def hi(c, i):
                    slot = c % FRING
                    to_hi(base + c + 6 * i, slot, use0(slot) + c // FRING + i, PANEL, (BASE_MOD[0] + c) % HRING)

                def step(s0, i):
                    silu(s0, i)
                    if s0 < n - 1:
                        hi(3 * s0 + 3, i)
                        if s0 == 1:
                            middle()
                        hid_hi_op(s0, i)
                        hi(3 * s0 + 4, i)
                        if s0 < n - 2:
                            hi(3 * s0 + 5, i)
                    else:
                        hi(3 * n - 1, i)
                        hid_hi_op(s0, i)
                        last()

                if not ahead:
                    hi(0, 0)
                    hi(1, 0)
                start()
                hi(2, 0)
                step(0, 0)
                step(1, 0)
                reps = ffn_span(n)
                with act.Fori(0, reps) as i:
                    for u in (2, 3):
                        step(u, i)
                for s in range(2 + 2 * reps, n):
                    step(s, 0)

            BASE_MOD = [0]

            def first_hi(base, use0):
                for c in range(2):
                    to_hi(base + c, c, use0[c], PANEL, (base + c) % HRING)

            mixer(0)
            first_hi(DENSE_BASE, DENSE_USE0)
            norm(1)
            norm_hi(1)

            def dense_silu(s0, i):
                c = (3 * s0 - 1 if s0 else 0) + 2
                act.wait_ge(panel_used, DENSE_BASE + c + 6 * i)
                if s0 >= 2:
                    act.wait_ge(S["hid_done"], s0 + 2 * i - 1)
                nc.scalar.activation(ar(A_SG + (s0 % 2) * 512, 512), pairs[s0 % 2][:, 0:512], ACT.Silu).then_inc(S["gu_silu"], 1)

            def dense_hid_hi(s0, i):
                act.wait_ge(S["hid_done"], s0 + 2 * i + 1)
                if s0 >= 2:
                    act.wait_ge(panel_used, DENSE_BASE + 3 * (s0 - 2) + 4 + 6 * i + 1)
                o = (s0 % 2) * 512
                nc.scalar.activation(act_hi[:, o:o + 512], ar(A_HID + o, 512), ACT.Copy).then_inc(S["hid_hi_done"], 1)

            BASE_MOD[0] = DENSE_BASE % HRING
            ffn_stream(DENSE_BASE, lambda s: DENSE_USE0[s], DENSE_STEPS, dense_silu, dense_hid_hi, True)

            mixer(1)
            act.wait_ge(param_in, 32)
            nc.scalar.activation(rt_hi[:, :], W("router", 0, 64), ACT.Copy).then_inc(S["router_hi"], 1)
            first_hi(EXP_BASE, EXP_USE0)
            norm(3)
            norm_hi(3)
            act.wait_ge(S["normed"], 8)
            nc.scalar.activation(act_hi[:, :], mrg[:, :], ACT.Copy).then_inc(S["hN_hi_done"], 1)
            act.wait_ge(S["routed_T"], 1)
            nc.scalar.activation(arena[0:8, A_MISC:A_MISC + 256], aux[0:8, 1024:1280], ACT.Copy).then_inc(S["routed_copied"], 1)
            act.wait_ge(S["route_read"], 1)
            nc.scalar.activation(small[:, 12:14], small[:, 10:12], ACT.Exp).then_inc(S["route_exp"], 1)

            def hx_hi(j):
                act.wait_ge(S["gathered"], j + 1)
                nc.scalar.activation(hT_hi[:, 0:4, :].rearrange("p k t -> p (k t)"), aux[:, 1024:2048], ACT.Copy)\
                   .then_inc(S["hx_hi_done"], 1)

            def expert(j, first=False):
                base = EXP_BASE + j * EXP_PANELS
                d0 = DENSE_STEPS + j * EXP_STEPS

                def silu(s0, i):
                    c = (3 * s0 - 1 if s0 else 0) + 2
                    act.wait_ge(panel_used, base + c + 6 * i)
                    act.wait_ge(S["hid_done"], d0 + s0 + 2 * i - 1)
                    nc.scalar.activation(ar(A_SG + (s0 % 2) * 512, STEP_F), pairs[s0 % 2][:, 0:STEP_F], ACT.Silu)\
                       .then_inc(S["gu_silu"], 1)

                def hid_hi_op(s0, i):
                    act.wait_ge(S["hid_turned"], j * EXP_STEPS + s0 + 2 * i + 1)
                    if s0 >= 2:
                        act.wait_ge(panel_used, base + 3 * (s0 - 2) + 5 + 6 * i)
                    nc.scalar.activation(hid_hi[:, s0 % 2, :], pairs[s0 % 2][:, 512:512 + STEP_F], ACT.Copy)\
                       .then_inc(S["hid_hi_done"], 1)

                def pickT_copy():
                    act.wait_ge(S["pick_turned"], j + 1)
                    nc.scalar.activation(pickT[:, :, :].rearrange("p b t -> p (b t)"), aux[:, 1024:1280], ACT.Copy)\
                       .then_inc(S["pickT_done"], 1)

                ffn_stream(base, lambda s: EXP_USE0[s] + (EXP_PANELS // FRING) * j, EXP_STEPS, silu, hid_hi_op, first,
                           (lambda: None) if first else (lambda: output_hi(j - 1)), pickT_copy, lambda: hx_hi(j + 1))

            def output_hi(j):
                act.wait_ge(panel_used, EXP_BASE + (j + 1) * EXP_PANELS)
                nc.scalar.activation(hT_hi[:, 4:8, :].rearrange("p k t -> p (k t)"), aux[:, 0:1024], ACT.Copy)\
                   .then_inc(S["oe_hi_done"], 1)

            BASE_MOD[0] = EXP_BASE % HRING
            hx_hi(0)
            expert(0, True)
            with act.Fori(1, NE) as j:
                expert(j)
            act.wait_ge(S["meta_done"], 1)
            m = act.value_load(meta[0:1, 0:1], min_val=0, max_val=EXTRA)
            with act.If(m > 0):
                with act.Fori(NE, m + NE) as j:
                    expert(j)
            output_hi(m + (NE - 1))
            warm_sqrt()
            act.wait_ge(S["extra_done"], 1)
            for b in range(NB):
                nc.scalar.activation(hN[:, b, :], x[:, b, :], ACT.Square, accum_out=small[:, b:b + 1]).then_inc(S["squared"], 1)
            act.wait_ge(S["meaned"], 5)
            nc.scalar.activation(small[:, 4:6], small[:, 2:4], ACT.Sqrt).then_inc(S["rooted"], 1)

        @block.tensor
        def _(pe):
            def passes(hi, lo, rhi, rlo):
                return ((hi, rlo), (lo, rhi), (hi, rhi))

            def split_mm(out, a, b, first, last=False):
                for n, (l, r) in enumerate(((a[0], b[1]), (a[1], b[0]), (a[0], b[0]))):
                    ins = pe.matmul(out, l, r, start=first and n == 0, stop=last and n == 2, skip_group_check=True)
                return ins

            def weights(h, width):
                return (hi_ring[:, h, 0:4 * width].rearrange("p (k n) -> p k n", n=width),
                        lo_ring[:, h, 0:4 * width].rearrange("p (k n) -> p k n", n=width))

            def norm(n):
                if n == 0:
                    pe.wait_ge(ident_in, 16)
                for b in range(NB):
                    pe.wait_ge(S["normed"], 2 * n + b + 1)
                    for k in range(KT):
                        ins = pe.transpose(aux[:, k * T + b * 128:k * T + (b + 1) * 128], hN[:, b, k * 128:(k + 1) * 128],
                                           C("ident"))
                        if b == NB - 1 and k % 2:
                            ins.then_inc(S["turned"], 1)

            def mixer(L):
                p = [MIX_BASE[L]]
                norm(2 * L)

                def free(name):
                    q = CH_INDEX[name]
                    if q >= 2:
                        pe.wait_ge(*ev(L, CHUNKS[q - 2][0]))

                def panel(width, body):
                    pe.wait_ge(lo_ready, p[0] + 1)
                    body(weights(p[0] % HRING, width)).then_inc(panel_used, 1)
                    p[0] += 1

                def t_block(out, w, c0, kh, first):
                    for k in range(4):
                        ins = split_mm(out, (w[0][:, k, c0:c0 + 128], w[1][:, k, c0:c0 + 128]),
                                       (hT_hi[:, 4 * kh + k, :], hT_lo[:, 4 * kh + k, :]),
                                       first and k == 0, kh == 1 and k == 3)
                    return ins

                def n_block(out, w, c0, n, b, kh, first):
                    for k in range(4):
                        ins = split_mm(out, (hT_hi[:, 4 * kh + k, b * 128:(b + 1) * 128], hT_lo[:, 4 * kh + k, b * 128:(b + 1) * 128]),
                                       (w[0][:, k, c0:c0 + n], w[1][:, k, c0:c0 + n]), first and k == 0, kh == 1 and k == 3)
                    return ins

                def t_panel(name, kh, groups=4, width=512):
                    g = pair_of(name)
                    if kh == 0:
                        free(name)
                    if name == "a":
                        pe.wait_ge(S["hT_lo_done"], 8 * L + 2 * kh + 2)

                    def body(w):
                        for i in range(groups):
                            ins = t_block(g[:, i * T:(i + 1) * T], w, i * 128, kh, kh == 0 and i % 2 == 0)
                        if name == "xbc1":
                            for b in range(NB):
                                ins = n_block(g[:, 512 + b * 8:520 + b * 8], w, 256, 8, b, kh, kh == 0 and b == 0)
                        return ins
                    panel(width, body)

                def t_chunk(name, groups=4, width=512):
                    for kh in range(2):
                        t_panel(name, kh, groups, width)

                t_chunk("a")
                t_chunk("gt")
                free("kiwi")
                for kh in range(2):
                    def body(w):
                        for b in range(NB):
                            ins = n_block(pair_of("kiwi")[:, b * 40:(b + 1) * 40], w, 0, 40, b, kh, kh == 0 and b == 0)
                        return ins
                    panel(40, body)
                free("kvqi")
                for kh in range(2):
                    def body(w):
                        g = pair_of("kvqi")
                        t_block(g[:, 0:256], w, 0, kh, kh == 0)
                        for b in range(NB):
                            n_block(g[:, 256 + b * 128:384 + b * 128], w, 128, 128, b, kh, False)
                        t_block(g[:, 512:768], w, 256, kh, kh == 0)
                        return t_block(g[:, 768:1024], w, 384, kh, False)
                    panel(512, body)
                t_chunk("q")
                t_chunk("pool")
                pe.wait_ge(*ev(L, "kiwi"))
                pe.wait_ge(S["hT_lo_done"], 4 * (2 * L + 1))
                for b in range(NB):
                    ins = pe.transpose(aux[:, b * 128:(b + 1) * 128], ar(A_KI + b * 128, 128), C("ident"))
                ins.then_inc(S["ki_turned"], 1)
                t_chunk("xbc0")
                if L == 0:
                    pe.wait_ge(const_in, 16)
                pe.wait_ge(S["ki_copied"], L + 1)
                pe.wait_ge(*ev(L, "q"))
                for i in range(8):
                    src = ar(A_IDX + i * T, T) if i < 3 else ar(A_QK + (i - 3) * T, T)
                    ins = pe.matmul(aux[:, i * T:(i + 1) * T], C("roti") if i < 3 else C("rotq"), src, start=True, stop=True)
                ins.then_inc(S["rotated"], 1)
                t_chunk("xbc1", 2, 264)
                t_panel("z", 0)
                free("lnsum")
                pe.wait_ge(S["conved"], 4 * CONV_W * (L + 1))
                for g in range(MG):
                    ins = pe.matmul(pair_of("lnsum")[:, 0:T], C("ones"), ar(A_CACC + g * T, T), start=(g == 0), stop=(g == 3))
                ins.then_inc(S["ln_summed"], 1)
                t_panel("z", 1)
                free("lnvar")
                pe.wait_ge(S["ln_squared"], L + 1)
                for g in range(MG):
                    ins = pe.matmul(pair_of("lnvar")[:, 0:T], C("ones"), ar(A_YPAD + g * T, T), start=(g == 0), stop=(g == 3))
                ins.then_inc(S["ln_varied"], 1)
                t_chunk("g2h0")
                t_chunk("g2h1")

                pe.wait_ge(S["roped"], L + 1)
                pe.matmul(aux[:, 0:256], C("swap"), ar(A_QK + 1024, 256), start=True, stop=True).then_inc(S["k_swapped"], 1)

                def index(b):
                    w = 128 * (b + 1)
                    if b == 0:
                        pe.wait_ge(S["k_copied"], L + 1)
                    else:
                        pe.wait_ge(S["relued"], 2 * L + 1)
                    for h in range(8):
                        r = 32 * (h % 4)
                        ins = pe.matmul(aux[:, 512 * (h % 4) + (h // 4) * w:512 * (h % 4) + (h // 4 + 1) * w],
                                        arena[r:r + 32, A_IDX + (h // 4) * T + b * 128:A_IDX + (h // 4) * T + (b + 1) * 128],
                                        arena[r:r + 32, A_IDX + 512:A_IDX + 512 + w], start=True, stop=True)
                    ins.then_inc(S["indexed"], 1)

                index(0)
                free("pooly")
                pe.wait_ge(S["pooled"], L + 1)
                for g in range(MG):
                    o = A_UPAD + g * (PPAD + T) + PPAD
                    ins = pe.matmul(pair_of("pooly")[:, g * T:(g + 1) * T], W("pool_w", g * 128, 128), ar(o, T),
                                    start=True, stop=True)
                ins.then_inc(S["pool_mixed"], 1)

                def branch_panel(i, h):
                    name = f"br{BR_ORDER[i]}h{h}"
                    pe.wait_ge(S["branch_lo"], 4 * L + i + 1)
                    free(name)

                    def body(w):
                        for g in range(4):
                            for k in range(4):
                                o = (i % 2) * 1024 + k * T
                                ins = split_mm(pair_of(name)[:, g * T:(g + 1) * T],
                                               (w[0][:, k, g * 128:(g + 1) * 128], w[1][:, k, g * 128:(g + 1) * 128]),
                                               (act_hi[:, o:o + T], act_lo[:, o:o + T]), k == 0 and g % 2 == 0, k == 3)
                        return ins
                    panel(512, body)

                branch_panel(0, 0)
                index(1)
                branch_panel(0, 1)
                t_panel("g0h0", 0)

                def logits(u):
                    j, b = u % 4, u // 4
                    w = 128 * (b + 1)
                    pe.wait_ge(S["relued"], 2 * L + 2)
                    if u:
                        pe.wait_ge(S["logits_read"], 8 * L + u)
                    for r in range(2):
                        kv = j // 2
                        ko = A_QK + 1024 if kv == r else A_KI
                        ins = pe.matmul(aux[:, r * 512:r * 512 + w],
                                        arena[64 * r:64 * r + 64, A_QK + j * T + b * 128:A_QK + j * T + (b + 1) * 128],
                                        arena[64 * r:64 * r + 64, ko:ko + w], start=True, stop=True)
                    ins.then_inc(S["logits_done"], 1)

                def attend(u):
                    j, b = u % 4, u // 4
                    nb = b + 1
                    pe.wait_ge(S["probs_done"], 8 * L + u + 1)
                    for r in range(2):
                        for s in range(nb):
                            o = 1024 + (r * nb + s) * 128
                            ins = pe.transpose(aux[:, o:o + 128], ar(A_CACC + 512 + r * 256 + s * 128, 128), C("ident"))
                    ins.then_inc(S["probs_turned"], 1)
                    pe.wait_ge(S["probs_copied"], 8 * L + u + 1)
                    if b:
                        pe.wait_ge(S["att_copied"], 8 * L + j + 1)
                    o = 1536 + j * 128
                    for r in range(2):
                        for s in range(nb):
                            v = ar(A_V + s * 128 + (j // 2) * 64, 64)
                            ins = pe.matmul(aux[64 * r:64 * r + 64, o:o + 128], v, ar(A_YPAD + (r * nb + s) * 128, 128),
                                            start=(s == 0), stop=(s == nb - 1))
                    ins.then_inc(S["attended"], 1)

                beside = [lambda: t_panel("g0h0", 1), lambda: t_panel("g0h1", 0), lambda: t_panel("g0h1", 1),
                          lambda: branch_panel(1, 0), lambda: branch_panel(1, 1),
                          lambda: t_panel("g1h0", 0), lambda: t_panel("g1h0", 1), lambda: t_panel("g1h1", 0)]
                for u in range(8):
                    logits(u)
                    beside[u]()
                    attend(u)

                pe.wait_ge(S["xbc_done"], L + 1)
                for b in range(NB):
                    for g in range(MG):
                        ins = pe.transpose(aux[:, b * 512 + g * 128:b * 512 + (g + 1) * 128],
                                           ar(A_XBC + g * T + b * 128, 128), C("ident"))
                ins.then_inc(S["xs_turned"], 1)
                pe.wait_ge(S["att_copied"], 8 * (L + 1))
                for g in range(2):
                    r, o = 64 * g, 1024 + 512 * g
                    bT, cT = A_XBC + 4 * T, A_XBC + 5 * T
                    pe.matmul(aux[:, o:o + 256], arena[r:r + 64, bT:bT + 128], arena[r:r + 64, cT:cT + 256], start=True, stop=True)
                    ins = pe.matmul(aux[:, o + 256:o + 384], arena[r:r + 64, bT + 128:bT + 256],
                                    arena[r:r + 64, cT + 128:cT + 256], start=True, stop=True)
                ins.then_inc(S["cb_done"], 1)
                t_panel("g1h1", 1)
                da = ar3(A_MISC + 32, 2, 8)
                pe.wait_ge(S["dt_done"], L + 1)
                pe.wait_ge(S["xd_done"], L + 1)
                pe.matmul(aux[:, 0:8], C("tri"), da[:, 0, :], start=True, stop=True)
                pe.matmul(aux[:, 8:16], C("ones"), da[:, 0, :], start=True, stop=False)
                pe.matmul(aux[:, 8:16], C("tri"), da[:, 1, :], start=False, stop=True).then_inc(S["acol_done"], 1)

                def arows(g):
                    if g == 0:
                        pe.wait_ge(S["acol_read"], L + 1)
                    else:
                        pe.wait_ge(S["arow_read"], 8 * L + 4)
                    for i in range(4):
                        h = 4 * g + i
                        o = i * 256
                        pe.matmul(aux[:, o:o + 256], da[:, 0, h:h + 1].broadcast_to([128, 128]),
                                  consts[:, CONSTS["tri"][0]:CONSTS["tri"][0] + 256], start=True, stop=False)
                        ins = pe.matmul(aux[:, o + 128:o + 256], da[:, 1, h:h + 1].broadcast_to([128, 128]), C("tri"),
                                        start=False, stop=True)
                    ins.then_inc(S["arow_done"], 1)

                def yhead(h):
                    pe.wait_ge(S["mixm_done"], 8 * L + h + 1)
                    if h == 0:
                        pe.wait_ge(S["cbm_done"], L + 1)
                    r, o = 64 * (h % 2), 1024 + (h // 2) * 256
                    m = A_P + 1024 + (h % 2) * 384
                    pe.matmul(aux[r:r + 64, o:o + 256], ar(A_P + h * 64, 64), ar(m, 256), start=True, stop=False)
                    ins = pe.matmul(aux[r:r + 64, o + 128:o + 256], ar(A_P + 512 + h * 64, 64), ar(m + 256, 128),
                                    start=False, stop=True)
                    ins.then_inc(S["y_done"], 1)

                arows(0)
                beside = [lambda: branch_panel(2, 0), lambda: branch_panel(2, 1), lambda: t_panel("g3h0", 0),
                          lambda: t_panel("g3h0", 1)]
                for k in range(4):
                    beside[k]()
                    if k == 1:
                        arows(1)
                    yhead(2 * k)
                    yhead(2 * k + 1)
                t_panel("g3h1", 0)
                free("rmsum")
                pe.wait_ge(S["rms_squared"], L + 1)
                for g in range(MG):
                    ins = pe.matmul(pair_of("rmsum")[:, 0:T], C("ones"), ar(A_P + g * T, T), start=(g == 0), stop=(g == 3))
                ins.then_inc(S["rms_summed"], 1)
                t_panel("g3h1", 1)
                branch_panel(3, 0)
                branch_panel(3, 1)
                for h in range(2):
                    name = f"out{h}"
                    free(name)
                    for kh in range(2):
                        pe.wait_ge(S["merged_lo"], 2 * L + kh + 1)

                        def body(w):
                            for b in range(NB):
                                for k in range(4):
                                    o = (4 * kh + k) * T + b * 128
                                    ins = split_mm(pair_of(name)[:, b * 512:(b + 1) * 512],
                                                   (act_hi[:, o:o + 128], act_lo[:, o:o + 128]),
                                                   (w[0][:, k, :], w[1][:, k, :]), kh == 0 and k == 0, kh == 1 and k == 3)
                            return ins
                        panel(512, body)

            def ffn_stream(n, up, down, turn, after_b0=lambda: None, after_a1=lambda: None, after_d0=lambda: None):
                def step(s0, i):
                    up(s0, i, 0)
                    if s0 == 1:
                        after_a1()
                    up(s0, i, 1)
                    if s0 == 0:
                        after_b0()
                    else:
                        down(s0 - 1, i)
                    if s0 == 1:
                        after_d0()
                    if s0 < n - 1:
                        turn(s0, i)

                step(0, 0)
                step(1, 0)
                reps = ffn_span(n)
                with pe.Fori(0, reps) as i:
                    for u in (2, 3):
                        step(u, i)
                for s in range(2 + 2 * reps, n):
                    step(s, 0)

            mixer(0)
            norm(1)

            def dense_up(s0, i, kh):
                c = (3 * s0 - 1 if s0 else 0) + kh
                if kh == 0 and s0 >= 2:
                    pe.wait_ge(S["hid_done"], s0 + 2 * i - 1)
                if s0 == 0:
                    pe.wait_ge(S["hT_lo_done"], 4 + 2 * kh + 2)
                pe.wait_ge(lo_ready, DENSE_BASE + c + 6 * i + 1)
                w = weights((DENSE_BASE + c) % HRING, 512)
                for g in range(4):
                    for k in range(4):
                        ins = split_mm(pairs[s0 % 2][:, g * T:(g + 1) * T],
                                       (w[0][:, k, g * 128:(g + 1) * 128], w[1][:, k, g * 128:(g + 1) * 128]),
                                       (hT_hi[:, 4 * kh + k, :], hT_lo[:, 4 * kh + k, :]), kh == 0 and k == 0 and g % 2 == 0,
                                       kh == 1 and k == 3)
                ins.then_inc(panel_used, 1)

            def dense_down(s0, i):
                c = DENSE_PANELS - 1 if s0 == DENSE_STEPS - 1 else 3 * s0 + 4
                pe.wait_ge(S["hid_lo_done"], s0 + 2 * i + 1)
                pe.wait_ge(lo_ready, DENSE_BASE + c + 6 * i + 1)
                w = weights((DENSE_BASE + c) % HRING, D // 2)
                o = (s0 % 2) * 512
                for b in range(NB):
                    for half in range(2):
                        for k in range(2):
                            q = o + k * T + b * 128
                            ins = split_mm(aux[:, (2 * b + half) * 512:(2 * b + half + 1) * 512],
                                           (act_hi[:, q:q + 128], act_lo[:, q:q + 128]),
                                           (w[0][:, 2 * k + half, :], w[1][:, 2 * k + half, :]),
                                           s0 == 0 and k == 0, s0 == DENSE_STEPS - 1 and k == 1)
                ins.then_inc(panel_used, 1)

            ffn_stream(DENSE_STEPS, dense_up, dense_down, lambda s0, i: None)
            dense_down(DENSE_STEPS - 1, 0)

            mixer(1)
            norm(3)
            pe.wait_ge(S["hT_lo_done"], 16)
            pe.wait_ge(S["router_split"], 1)
            for k in range(KT):
                for n, (l, r) in enumerate(((rt_lo, hT_lo), (rt_lo, hT_hi), (rt_hi, hT_lo), (rt_hi, hT_hi))):
                    ins = pe.matmul(aux[0:8, 1024:1280], l[:, k * 8:k * 8 + 8], r[:, k, :], start=(k == 0 and n == 0),
                                    stop=(k == KT - 1 and n == 3))
            ins.then_inc(S["routed_T"], 1)
            pe.wait_ge(S["routed_copied"], 1)
            for b in range(NB):
                ins = pe.transpose(aux[:, b * 8:b * 8 + 8], arena[0:8, A_MISC + b * 128:A_MISC + (b + 1) * 128],
                                   consts[0:8, CONSTS["ident"][0]:CONSTS["ident"][0] + 8])
            ins.then_inc(S["routed"], 1)
            pe.wait_ge(S["masks_done"], 1)
            m0, m1 = ar(A_SCORE, 8), ar(A_SCORE + 8, 8)
            pe.matmul(aux[:, 512:520], C("strict"), m0, start=True, stop=True)
            pe.matmul(aux[:, 520:528], C("ones"), m0, start=True, stop=False)
            pe.matmul(aux[:, 520:528], C("strict"), m1, start=False, stop=True)
            pe.matmul(aux[:, 528:536], C("ones"), m0, start=True, stop=False)
            pe.matmul(aux[:, 528:536], C("ones"), m1, start=False, stop=True).then_inc(S["counted"], 1)

            def gather(j):
                pe.wait_ge(S["pick_done"], j + 1)
                for k in range(KT):
                    for b in range(NB):
                        for n, src in enumerate((act_lo, act_hi)):
                            ins = pe.matmul(aux[:, 1024 + k * 128:1024 + (k + 1) * 128], src[:, b * D + k * 128:b * D + (k + 1) * 128],
                                            pick[:, b, :], start=(b == 0 and n == 0), stop=(b == 1 and n == 1))
                ins.then_inc(S["gathered"], 1)

            def expert(j, first=False):
                base = EXP_BASE + j * EXP_PANELS
                d0 = DENSE_STEPS + j * EXP_STEPS

                def up(s0, i, kh):
                    c = (3 * s0 - 1 if s0 else 0) + kh
                    if kh == 0:
                        pe.wait_ge(S["hid_lo_done"], d0 + s0 + 2 * i - 1)
                    pe.wait_ge(lo_ready, base + c + 6 * i + 1)
                    w = weights((EXP_BASE + c) % HRING, 512)
                    for k in range(4):
                        a = (4 * kh + k) * 128
                        ins = split_mm(pairs[s0 % 2][:, 0:512], (hxh[:, a:a + 128], hxl[:, a:a + 128]),
                                       (w[0][:, k, :], w[1][:, k, :]), kh == 0 and k == 0, kh == 1 and k == 3)
                    ins.then_inc(panel_used, 1)

                def turn(s0, i):
                    pe.wait_ge(S["hid_done"], d0 + s0 + 2 * i + 1)
                    for k in range(2):
                        ins = pe.transpose(pairs[s0 % 2][:, 512 + k * 128:640 + k * 128],
                                           ar(A_HID + (s0 % 2) * 512 + k * 128, 128), C("ident"))
                    ins.then_inc(S["hid_turned"], 1)

                def down(s0, i):
                    c = EXP_PANELS - 1 if s0 == EXP_STEPS - 1 else 3 * s0 + 4
                    pe.wait_ge(S["hid_lo_done"], d0 + s0 + 2 * i + 1)
                    pe.wait_ge(lo_ready, base + c + 6 * i + 1)
                    w = weights((EXP_BASE + c) % HRING, 512)
                    for half in range(2):
                        for k in range(2):
                            ins = split_mm(aux[:, half * 512:(half + 1) * 512],
                                           (hid_hi[:, s0 % 2, k * 128:(k + 1) * 128], hid_lo[:, s0 % 2, k * 128:(k + 1) * 128]),
                                           (w[0][:, 2 * k + half, :], w[1][:, 2 * k + half, :]),
                                           s0 == 0 and k == 0, s0 == EXP_STEPS - 1 and k == 1)
                    ins.then_inc(panel_used, 1)

                pe.wait_ge(S["hx_lo_done"], j + 1)
                def turn_pick():
                    if not first:
                        pe.wait_ge(S["x_added"], 2 * j)
                    for b in range(NB):
                        ins = pe.matmul(aux[:, 1024 + b * 128:1152 + b * 128], pick[:, b, :], ident_r[:, :], start=True, stop=True)
                    ins.then_inc(S["pick_turned"], 1)

                if first:
                    ffn_stream(EXP_STEPS, up, down, turn, after_d0=turn_pick)
                else:
                    ffn_stream(EXP_STEPS, up, down, turn, lambda: scatter(j - 1, 0), lambda: scatter(j - 1, 1), turn_pick)
                pe.wait_ge(S["pickT_done"], j + 1)
                turn(EXP_STEPS - 1, 0)
                gather(j + 1)
                down(EXP_STEPS - 1, 0)

            def scatter(j, b):
                if b == 0:
                    pe.wait_ge(S["oe_lo_done"], j + 1)
                else:
                    pe.wait_ge(S["x_added"], 2 * j + 1)
                for half in range(2):
                    for n, src in enumerate((oel, oeh)):
                        ins = pe.matmul(aux[:, 1024 + half * 512:1536 + half * 512], pickT[:, b, :],
                                        src[:, half * 512:(half + 1) * 512], start=(n == 0), stop=(n == 1))
                ins.then_inc(S["scattered"], 1)

            hxh = hT_hi[:, 0:4, :].rearrange("p k t -> p (k t)")
            hxl = hT_lo[:, 0:4, :].rearrange("p k t -> p (k t)")
            oeh = hT_hi[:, 4:8, :].rearrange("p k t -> p (k t)")
            oel = hT_lo[:, 4:8, :].rearrange("p k t -> p (k t)")
            pe.wait_ge(S["hN_lo_done"], 1)
            pe.wait_ge(S["ident_done"], 1)
            gather(0)
            expert(0, True)
            with pe.Fori(1, NE) as j:
                expert(j)
            pe.wait_ge(S["meta_done"], 1)
            m = pe.value_load(meta[0:1, 0:1], min_val=0, max_val=EXTRA)
            with pe.If(m > 0):
                with pe.Fori(NE, m + NE) as j:
                    expert(j)
            scatter(m + (NE - 1), 0)
            scatter(m + (NE - 1), 1)

        @block.vector
        def _(dve):
            own = [0]

            def link(ins):
                own[0] += 1
                ins.then_inc(v_done, 1)
                dve.wait_ge(v_done, own[0])

            def to_lo(p, slot, cols, h):
                dve.wait_ge(hi_ready, p + 1)
                nc.vector.tensor_tensor(lo_ring[:, h, 0:cols], raw(slot)[:, 0:cols], hi_ring[:, h, 0:cols].bitcast(f32),
                                        ALU.subtract).then_inc(lo_ready, 1)

            MCOLS = mixer_cols()

            def norm(n):
                dve.wait_ge(S["squared"], 2 * n + 2)
                nc.vector.tensor_scalar(small[:, 2:4], small[:, 0:2], 1.0 / D, EPS, ALU.mult, ALU.add).then_inc(S["meaned"], 1)
                dve.wait_ge(S["rooted"], n + 1)
                link(nc.vector.reciprocal(small[:, 6:8], small[:, 4:6]))
                dve.wait_ge(gain_in, 16 * (n + 1))
                for b in range(NB):
                    nc.vector.scalar_tensor_tensor(hN[:, b, :], x[:, b, :], small[:, 6 + b:7 + b], gain[:, :], ALU.mult,
                                                   ALU.mult).then_inc(S["final_done"] if n == 4 else S["normed"], 1)

            def norm_lo(n):
                for j in range(4):
                    dve.wait_ge(S["hT_hi_done"], 4 * n + j + 1)
                    o = hT_lo[:, 2 * j:2 * j + 2, :].rearrange("p k t -> p (k t)")
                    i = hT_hi[:, 2 * j:2 * j + 2, :].rearrange("p k t -> p (k t)")
                    nc.vector.tensor_tensor(o, aux[:, j * 512:(j + 1) * 512], i.bitcast(f32), ALU.subtract)\
                      .then_inc(S["hT_lo_done"], 1)

            def mixer(L, add_dense=None):
                done = [0]

                def lo_upto(n):
                    while done[0] < min(n, MIX_PANELS):
                        i = done[0]
                        slot, _ = MSLOT[L][i]
                        p = MIX_BASE[L] + i
                        to_lo(p, slot, MCOLS[i], p % HRING)
                        done[0] += 1

                if L:
                    lo_upto(2)
                    add_dense()
                else:
                    nc.vector.memset(small[:, 44:45], 1.0).then_inc(S["one_set"], 1)
                upad = ar3(A_UPAD, 4, PPAD + T)
                ypad = ar3(A_YPAD, 4, CPAD + T)
                xpad = ar3(A_XBCP, 6, SPAD + T)
                nc.vector.memset(upad[:, :, 0:PPAD], 0.0)
                nc.vector.memset(ypad[:, :, 0:CPAD], 0.0)
                nc.vector.memset(xpad[:, :, 0:SPAD], 0.0).then_inc(S["pads_done"], 1)
                norm(2 * L)
                lo_upto(1)
                norm_lo(2 * L)
                dve.wait_ge(param_in, 16 * (L + 1))
                lo_upto(6)
                dve.wait_ge(*ev(L, "gt"))
                link(nc.vector.tensor_tensor(ypad[:, :, CPAD:], ar3(A_P, 4, T), ar3(A_P + 1024, 4, T), ALU.mult))
                c0 = 4 * CONV_W * L
                for t in range(CONV_W):
                    for g in range(MG):
                        i = t * MG + g
                        src = ypad[:, g, t:t + T]
                        dst = ar(A_CACC + g * T, T)
                        if t == 0:
                            ins = nc.vector.tensor_scalar(dst, src, W("conv_dw", g * CONV_W), W("conv_b", g), ALU.mult, ALU.add)
                        else:
                            dve.wait_ge(S["conved"], c0 + i - MG + 1)
                            ins = nc.vector.scalar_tensor_tensor(dst, src, W("conv_dw", g * CONV_W + t), dst, ALU.mult, ALU.add)
                        ins.then_inc(S["conved"], 1)
                        if i % 9 == 8:
                            lo_upto(min(done[0] + 1, CH_PANEL["g2h0"]))
                dve.wait_ge(S["ln_summed"], L + 1)
                mean = ar(A_MISC + 128, T)
                nc.vector.tensor_scalar(mean, pair_of("lnsum")[:, 0:T], 1.0 / MIX, None, ALU.mult).then_inc(emptied["D"], 1)
                dve.wait_ge(*ev(L, "lnsum"))
                cacc = ar3(A_CACC, 4, T)
                ins = nc.vector.tensor_tensor(cacc, cacc, mean.unsqueeze(1).broadcast_to([128, 4, T]), ALU.subtract)
                ins.then_inc(S["centred"], 1)
                mi = lambda o, n=16: ar(A_MISC + o, n)
                dve.wait_ge(*ev(L, "xbc1"))
                link(nc.vector.tensor_tensor(ar3(A_MISC + 16, 2, 8), ar3(A_MISC + 16, 2, 8),
                                             W("dt_bias", 0, 8).unsqueeze(1).broadcast_to([128, 2, 8]), ALU.add))
                nc.vector.scalar_tensor_tensor(mi(48), mi(16), -1.0, mi(16), ALU.mult, ALU.max).then_inc(S["dt_abs"], 1)
                if L == 0:
                    dve.wait_ge(const_in, 16)
                dve.wait_ge(S["rotated"], L + 1)
                for o, n, rot, cs, sn in ((A_IDX, 3, 0, "cosi", "sini"), (A_QK, 5, 3 * T, "cosq", "sinq")):
                    v = ar3(o, n, T)
                    r = ar3(A_P, n, T)
                    link(nc.vector.tensor_tensor(r, aux[:, rot:rot + n * T].rearrange("p (n t) -> p n t", t=T),
                                                 C(sn).unsqueeze(1).broadcast_to([128, n, T]), ALU.mult))
                    link(nc.vector.tensor_tensor(v, v, C(cs).unsqueeze(1).broadcast_to([128, n, T]), ALU.mult))
                    ins = nc.vector.tensor_tensor(v, v, r, ALU.add)
                    if o == A_QK:
                        ins.then_inc(S["roped"], 1)
                    else:
                        link(ins)
                        dve.wait_ge(S["dt_exp"], L + 1)
                        nc.vector.tensor_scalar(mi(64), mi(48), 1.0, None, ALU.add).then_inc(S["dt_plus"], 1)
                        lo_upto(19)
                dve.wait_ge(S["roped"], L + 1)
                lo_upto(20)
                dve.wait_ge(S["ln_varied"], L + 1)
                nc.vector.tensor_scalar(mean, pair_of("lnvar")[:, 0:T], 1.0 / MIX, EPS, ALU.mult, ALU.add)\
                  .then_inc(emptied["D"], 1)
                dve.wait_ge(S["ln_rooted"], L + 1)
                link(nc.vector.reciprocal(mean, mean))
                nc.vector.tensor_tensor(cacc, cacc, mean.unsqueeze(1).broadcast_to([128, 4, T]), ALU.mult)\
                  .then_inc(S["ln_scaled"], 1)
                lo_upto(21)
                s1, s2 = ar3(A_P, 4, PPAD + T), ar3(A_P + 4 * (PPAD + T), 4, PPAD + T)
                link(nc.vector.memset(ar(A_P, 8 * (PPAD + T)).rearrange("p (g t) -> p g t", t=PPAD + T)[:, :, 0:PPAD], 0.0))
                dve.wait_ge(*ev(L, "pool"))
                src = upad
                where = []
                for lv, dst in enumerate((s1, s2, s1, s2)):
                    sh = 1 << lv
                    link(nc.vector.tensor_tensor(dst[:, lv:4, PPAD:], src[:, lv:4, PPAD:], src[:, lv:4, PPAD - sh:PPAD + T - sh],
                                                 ALU.add))
                    where.append(dst)
                    src = dst
                lo_upto(22)
                for g in range(4):
                    w = 2 << g
                    s = where[g][:, g, :]
                    u = upad[:, g, :]
                    link(nc.vector.tensor_tensor(s[:, PPAD:PPAD + 16], s[:, PPAD:PPAD + 16],
                                                 consts[:, CONSTS["invcnt"][0] + 16 * g:CONSTS["invcnt"][0] + 16 * g + 16], ALU.mult))
                    nc.vector.tensor_tensor(u[:, PPAD:PPAD + 16], s[:, PPAD:PPAD + 16], u[:, PPAD:PPAD + 16], ALU.subtract)
                    ins = nc.vector.scalar_tensor_tensor(u[:, PPAD + 16:], s[:, PPAD + 16:], 1.0 / w, u[:, PPAD + 16:],
                                                         ALU.mult, ALU.subtract)
                ins.then_inc(S["pooled"], 1)
                dve.wait_ge(S["ln_sig"], L + 1)
                for g in range(MG):
                    ins = nc.vector.tensor_scalar(ar(A_CACC + g * T, T), ar(A_CACC + g * T, T), W("ln_g", g), W("ln_b", g),
                                                  ALU.mult, ALU.add)
                link(ins)
                nc.vector.tensor_tensor(ar(A_CACC, 1024), ar(A_CACC, 1024), ar(A_YPAD, 1024), ALU.mult).then_inc(S["branch_f"], 1)
                lo_upto(23)

                def branch_lo(i, src=A_UPAD):
                    dve.wait_ge(S["branch_hi"], 4 * L + i + 1)
                    o = (i % 2) * 1024
                    nc.vector.tensor_tensor(act_lo[:, o:o + 1024], ar(src, 1024), act_hi[:, o:o + 1024].bitcast(f32),
                                            ALU.subtract).then_inc(S["branch_lo"], 1)

                def merge(i, h):
                    name = f"br{BR_ORDER[i]}h{h}"
                    g = pair_of(name)
                    dve.wait_ge(panel_used, used_after(L, name))
                    dve.wait_ge(*ev(L, f"g{BR_ORDER[i]}h{h}"))
                    gates = ar(A_GATES + h * 1024, 1024)
                    dst = mrg[:, h * 1024:(h + 1) * 1024]
                    if i == 0:
                        nc.vector.tensor_tensor(dst, g[:, :], gates, ALU.mult).then_inc(emptied["D"], 1)
                    else:
                        link(nc.vector.tensor_tensor(g[:, :], g[:, :], gates, ALU.mult))
                        nc.vector.tensor_tensor(dst, g[:, :], dst, ALU.add).then_inc(emptied["D"], 1)

                def score(b):
                    w = 128 * (b + 1)
                    sc = ar(A_SCORE + 128 * b, w)
                    dve.wait_ge(S["relued"], 2 * L + b + 1)
                    far = CONSTS["far"][0] + 256
                    for h in range(8):
                        ins = nc.vector.scalar_tensor_tensor(sc, ar(A_P + h * w, w), ar(A_MISC + 8 * b + h, 1),
                                                             consts[:, far - w:far] if h == 0 else sc, ALU.mult, ALU.add)
                        if h < 7:
                            link(ins)
                        else:
                            ins.then_inc(S["scored"], 1)
                            dve.wait_ge(S["scored"], 2 * L + b + 1)

                def take(b, rounds):
                    sc = ar(A_SCORE + 128 * b, 128 * (b + 1))
                    best = small[:, 16:24]
                    for _ in range(rounds):
                        link(nc.vector.max(best, sc))
                        link(nc.vector.match_replace(sc, best, sc, TAKEN))

                def topk_mask(b):
                    w = 128 * (b + 1)
                    mask = ar(A_MASK + 128 * b, w)
                    link(nc.vector.tensor_scalar(mask, ar(A_SCORE + 128 * b, w), TAKEN, None, ALU.is_equal))
                    link(nc.vector.tensor_tensor(mask[:, w - 128:w], mask[:, w - 128:w], C("causal"), ALU.mult))
                    link(nc.vector.tensor_scalar(mask, mask, 1.0, -FAR, ALU.subtract, ALU.mult))

                branch_lo(0, A_CACC)
                lo_upto(24)
                branch_lo(1)
                score(0)
                take(0, 2)
                merge(0, 0)
                lo_upto(25)
                take(0, TOPK // 8 - 2)
                topk_mask(0)
                merge(0, 1)
                lo_upto(26)

                def dt_finish():
                    dve.wait_ge(S["dt_plus"], L + 1)
                    link(nc.vector.tensor_scalar(mi(384), mi(64), 1.0, None, ALU.subtract))
                    dve.wait_ge(S["dt_ln"], L + 1)
                    link(nc.vector.tensor_scalar(mi(64), mi(384), 0.0, None, ALU.is_equal))
                    nc.vector.tensor_tensor(mi(80), mi(80), mi(64), ALU.add)
                    link(nc.vector.tensor_tensor(mi(384), mi(384), mi(64), ALU.add))
                    link(nc.vector.reciprocal(mi(384), mi(384)))
                    link(nc.vector.tensor_tensor(mi(80), mi(80), mi(384), ALU.mult))
                    link(nc.vector.tensor_tensor(mi(80), mi(80), mi(48), ALU.mult))
                    link(nc.vector.scalar_tensor_tensor(mi(16), mi(16), 0.0, mi(80), ALU.max, ALU.add))
                    dve.wait_ge(S["a_exp"], L + 1)
                    nc.vector.scalar_tensor_tensor(ar3(A_MISC + 32, 2, 8), ar3(A_MISC + 16, 2, 8), -1.0,
                                                   mi(112, 8).unsqueeze(1).broadcast_to([128, 2, 8]), ALU.mult, ALU.mult)\
                      .then_inc(S["dt_done"], 1)

                taps = [(t, g) for t in range(SSM_W) for g in range(6)]

                def ssm_taps(k):
                    for _ in range(k):
                        t, g = taps.pop(0)
                        src, dst = xpad[:, g, t:t + T], ar(A_XBC + g * T, T)
                        i = t * 6 + g
                        if t == 0:
                            ins = nc.vector.tensor_scalar(dst, src, W("ssm_w", g * SSM_W), W("ssm_b", g), ALU.mult, ALU.add)
                        else:
                            dve.wait_ge(S["xbc_tap"], 24 * L + i - 5)
                            ins = nc.vector.scalar_tensor_tensor(dst, src, W("ssm_w", g * SSM_W + t), dst, ALU.mult, ALU.add)
                        ins.then_inc(S["xbc_tap"], 1)

                for u in range(8):
                    j, b = u % 4, u // 4
                    w = 128 * (b + 1)
                    lo_upto(UNIT_PANEL + u + 2)
                    dve.wait_ge(S["logits_done"], 8 * L + u + 1)
                    lg = ar3(A_CACC, 2, 256)[:, :, 0:w]
                    pr = ar3(A_CACC + 512, 2, 256)[:, :, 0:w]
                    nc.vector.scalar_tensor_tensor(lg, aux[:, 0:1024].rearrange("p (r c) -> p r c", r=2)[:, :, 0:w], 0.125,
                                                   ar(A_MASK + 128 * b, w).unsqueeze(1).broadcast_to([128, 2, w]),
                                                   ALU.mult, ALU.add).then_inc(S["logits_read"], 1)
                    dve.wait_ge(S["logits_read"], 8 * L + u + 1)
                    nc.vector.tensor_reduce(mi(96, 2), lg, AX.X, ALU.max, negate=True).then_inc(S["negmax_done"], 1)
                    if u < 6:
                        ssm_taps(4)
                    dve.wait_ge(S["exped"], 8 * L + u + 1)
                    link(nc.vector.reciprocal(mi(100, 2), mi(98, 2)))
                    nc.vector.tensor_tensor(pr, pr, mi(100, 2).unsqueeze(2).broadcast_to([128, 2, w]), ALU.mult)\
                      .then_inc(S["probs_done"], 1)
                    if u == 0:
                        score(1)
                    elif u < 4:
                        take(1, (3, 3, 2)[u - 1])
                        if u == 3:
                            topk_mask(1)
                    elif u < 6:
                        merge(1, u - 4)
                        if u == 5:
                            dt_finish()
                    elif u == 6:
                        dve.wait_ge(S["xbc_sig"], L + 1)
                        nc.vector.tensor_tensor(ar(A_XBC, 1536), ar(A_XBC, 1536), ar(A_P, 1536), ALU.mult).then_inc(S["xbc_done"], 1)
                lo_upto(HEAD_PANEL + 1)
                dve.wait_ge(S["xs_turned"], L + 1)
                for b in range(NB):
                    dst = ar3(A_P + b * 512, 8, 64)
                    ins = nc.vector.tensor_tensor(dst, aux[:, b * 512:(b + 1) * 512].rearrange("p (h d) -> p h d", d=64),
                                                  mi(16 + 8 * b, 8).unsqueeze(2).broadcast_to([128, 8, 64]), ALU.mult)
                ins.then_inc(S["xd_done"], 1)
                branch_lo(2)
                dve.wait_ge(S["cb_done"], L + 1)
                for g in range(2):
                    o, c = A_CACC + 384 * g, 1024 + 512 * g
                    nc.vector.tensor_tensor(ar(o, 128), aux[:, c:c + 128], C("tri"), ALU.mult)
                    nc.vector.tensor_copy(ar(o + 128, 128), aux[:, c + 128:c + 256])
                    ins = nc.vector.tensor_tensor(ar(o + 256, 128), aux[:, c + 256:c + 384], C("tri"), ALU.mult)
                ins.then_inc(S["cbm_done"], 1)
                dve.wait_ge(S["acol_done"], L + 1)
                nc.vector.tensor_copy(mi(64), aux[:, 0:16]).then_inc(S["acol_read"], 1)
                dve.wait_ge(S["acol_read"], L + 1)
                dve.wait_ge(S["cbm_done"], L + 1)

                def seg(h):
                    dve.wait_ge(S["arow_done"], 2 * L + h // 4 + 1)
                    if h >= 2:
                        dve.wait_ge(S["mixm_done"], 8 * L + h - 1)
                    e, o = A_YPAD + (h % 2) * 384, (h % 4) * 256
                    nc.vector.tensor_scalar(ar(e, 256), aux[:, o:o + 256], mi(64 + h, 1), 0.0, ALU.subtract, ALU.min)
                    nc.vector.tensor_scalar(ar(e + 256, 128), aux[:, o + 128:o + 256], mi(72 + h, 1), 0.0, ALU.subtract,
                                            ALU.min).then_inc(S["arow_read"], 1)

                def mixm(h):
                    dve.wait_ge(S["decay_exp"], 8 * L + h + 1)
                    if h >= 2:
                        dve.wait_ge(S["y_done"], 8 * L + h - 1)
                    e, q = A_YPAD + (h % 2) * 384, A_P + 1024 + (h % 2) * 384
                    nc.vector.tensor_tensor(ar(q, 384), ar(e, 384), ar(A_CACC + 384 * (h // 4), 384), ALU.mult)\
                      .then_inc(S["mixm_done"], 1)

                lo_upto(HEAD_PANEL + 2)
                seg(0)
                for h in range(8):
                    if h < 7:
                        seg(h + 1)
                    mixm(h)
                    if h % 2 == 1:
                        lo_upto(HEAD_PANEL + h // 2 + 3)
                    if h == 1 or h == 3:
                        merge(2, h // 2)
                    if h == 5:
                        dve.wait_ge(S["z_sig"], L + 1)
                        nc.vector.tensor_tensor(ar(A_Z, 1024), ar(A_Z, 1024), ar(A_XBCP, 1024), ALU.mult).then_inc(S["z_done"], 1)
                dve.wait_ge(S["z_done"], L + 1)
                y = ar3(A_XBCP, 4, T)
                for g in range(MG):
                    dve.wait_ge(S["y_done"], 8 * L + 8)
                    ins = nc.vector.scalar_tensor_tensor(y[:, g, :], ar(A_XBC + g * T, T), W("dskip", g),
                                                         aux[:, 1024 + g * T:1024 + (g + 1) * T], ALU.mult, ALU.add)
                link(ins)
                dve.wait_ge(S["z_done"], L + 1)
                nc.vector.tensor_tensor(ar(A_XBCP, 1024), ar(A_XBCP, 1024), ar(A_Z, 1024), ALU.mult).then_inc(S["gated"], 1)
                lo_upto(40)
                lo_upto(41)
                dve.wait_ge(S["rms_summed"], L + 1)
                nc.vector.tensor_scalar(mean, pair_of("rmsum")[:, 0:T], 1.0 / MIX, EPS, ALU.mult, ALU.add)\
                  .then_inc(emptied["D"], 1)
                dve.wait_ge(S["rms_rooted"], L + 1)
                link(nc.vector.reciprocal(mean, mean))
                dve.wait_ge(S["gated"], L + 1)
                for g in range(MG):
                    ins = nc.vector.scalar_tensor_tensor(ar(A_UPAD + g * T, T), y[:, g, :], W("ssm_norm", g), mean,
                                                         ALU.mult, ALU.mult)
                ins.then_inc(S["branch_f"], 1)
                branch_lo(3)
                lo_upto(43)
                for h in range(2):
                    merge(3, h)
                    dve.wait_ge(S["merged_hi"], 2 * L + h + 1)
                    nc.vector.tensor_tensor(act_lo[:, h * 1024:(h + 1) * 1024], mrg[:, h * 1024:(h + 1) * 1024],
                                            act_hi[:, h * 1024:(h + 1) * 1024].bitcast(f32), ALU.subtract)\
                      .then_inc(S["merged_lo"], 1)
                    lo_upto(44 + h)
                lo_upto(46)
                for h in range(2):
                    if h:
                        base = EXP_BASE if L else DENSE_BASE
                        for c in range(2):
                            to_lo(base + c, c, PANEL, (base + c) % HRING)
                    name = f"out{h}"
                    dve.wait_ge(panel_used, used_after(L, name))
                    xs = x[:, :, h * 512:(h + 1) * 512]
                    nc.vector.tensor_tensor(xs, pair_of(name)[:, :].rearrange("p (b n) -> p b n", b=NB), xs, ALU.add)\
                      .then_inc(emptied["D"], 1)

            def ffn_stream(base, mod, n, hid, hid_lo_op, ahead=False, start=lambda: None, after_hid0=lambda: None,
                           after_d0=lambda: None, after_a3=lambda: None, last=lambda: None):
                def lo(c, i):
                    to_lo(base + c + 6 * i, c % FRING, PANEL, (mod + c) % HRING)

                def step(s0, i):
                    hid(s0, i)
                    if s0 == 0:
                        after_hid0()
                    if s0 < n - 1:
                        lo(3 * s0 + 3, i)
                        hid_lo_op(s0, i)
                        lo(3 * s0 + 4, i)
                        if s0 == 0:
                            after_d0()
                        if s0 < n - 2:
                            lo(3 * s0 + 5, i)
                        if s0 == 1:
                            after_a3()
                    else:
                        lo(3 * n - 1, i)
                        hid_lo_op(s0, i)
                        last()

                if not ahead:
                    lo(0, 0)
                    lo(1, 0)
                start()
                lo(2, 0)
                step(0, 0)
                step(1, 0)
                reps = ffn_span(n)
                with dve.Fori(0, reps) as i:
                    for u in (2, 3):
                        step(u, i)
                for s in range(2 + 2 * reps, n):
                    step(s, 0)

            mixer(0)
            norm(1)
            norm_lo(1)

            def dense_hid(s0, i):
                dve.wait_ge(S["gu_silu"], s0 + 2 * i + 1)
                o = (s0 % 2) * 512
                if s0 >= 2:
                    dve.wait_ge(S["hid_hi_done"], s0 + 2 * i - 1)
                nc.vector.tensor_tensor(ar(A_HID + o, 512), pairs[s0 % 2][:, 512:1024], ar(A_SG + o, 512), ALU.mult)\
                  .then_inc(S["hid_done"], 1)

            def dense_hid_lo(s0, i):
                dve.wait_ge(S["hid_hi_done"], s0 + 2 * i + 1)
                o = (s0 % 2) * 512
                nc.vector.tensor_tensor(act_lo[:, o:o + 512], ar(A_HID + o, 512), act_hi[:, o:o + 512].bitcast(f32),
                                        ALU.subtract).then_inc(S["hid_lo_done"], 1)

            ffn_stream(DENSE_BASE, DENSE_BASE % HRING, DENSE_STEPS, dense_hid, dense_hid_lo, True)

            def add_dense():
                dve.wait_ge(panel_used, DENSE_BASE + DENSE_PANELS)
                for b in range(NB):
                    ins = nc.vector.tensor_tensor(x[:, b, :], aux[:, b * 1024:(b + 1) * 1024], x[:, b, :], ALU.add)
                ins.then_inc(S["dense_added"], 1)

            mixer(1, add_dense)
            dve.wait_ge(S["router_hi"], 1)
            nc.vector.tensor_tensor(rt_lo[:, :], W("router", 0, 64), rt_hi[:, :].bitcast(f32), ALU.subtract)\
              .then_inc(S["router_split"], 1)
            norm(3)
            norm_lo(3)
            dve.wait_ge(S["hN_hi_done"], 1)
            nc.vector.tensor_tensor(act_lo[:, :], mrg[:, :], act_hi[:, :].bitcast(f32), ALU.subtract).then_inc(S["hN_lo_done"], 1)
            R = A_SCORE
            mask, lgt, oh0, key, oh1, l2 = (ar3(R + 16 * k, 2, 8) for k in range(6))
            comb_t = ar3(R + 96, 2, SLOTS)
            pos_t = ar3(R + 96 + 2 * SLOTS, 2, SLOTS)
            p1 = ar3(R + 96 + 4 * SLOTS, 2, 8)
            sel = ar(R + 200, 8)
            cum = ar(R + 208, 8)
            over = ar(R + 216, 8)
            tmp = ar3(R + 224, 2, 8)
            rev = C("rev8").unsqueeze(1).broadcast_to([128, 2, 8])

            def make_pick(j):
                for b in range(NB):
                    ins = nc.vector.tensor_scalar(pick[:, b, :], C("iota"), arena[:, bass.ds(R + 96 + 2 * SLOTS + b * SLOTS + j, 1)],
                                                  None, ALU.is_equal)
                ins.then_inc(S["pick_done"], 1)

            def first_max(src, oh, peak, at):
                link(nc.vector.tensor_reduce(peak, src, AX.X, ALU.max))
                link(nc.vector.tensor_tensor(key, src, peak.unsqueeze(2).broadcast_to([128, 2, 8]), ALU.is_equal))
                link(nc.vector.tensor_tensor(key, key, rev, ALU.mult))
                link(nc.vector.tensor_reduce(at, key, AX.X, ALU.max))
                link(nc.vector.tensor_tensor(oh, key, at.unsqueeze(2).broadcast_to([128, 2, 8]), ALU.is_equal))

            dve.wait_ge(S["routed"], 1)
            link(nc.vector.tensor_copy(lgt, aux[:, 0:16].rearrange("p (b e) -> p b e", e=8)))
            first_max(lgt, oh0, small[:, 26:28], small[:, 28:30])
            link(nc.vector.scalar_tensor_tensor(l2, oh0, FAR, lgt, ALU.mult, ALU.add))
            first_max(l2, oh1, small[:, 30:32], small[:, 28:30])
            nc.vector.tensor_tensor(small[:, 10:12], small[:, 30:32], small[:, 26:28], ALU.subtract).then_inc(S["route_read"], 1)
            nc.vector.tensor_tensor(mask, oh0, oh1, ALU.add).then_inc(S["masks_done"], 1)
            dve.wait_ge(S["route_exp"], 1)
            link(nc.vector.tensor_scalar(small[:, 32:34], small[:, 12:14], 1.0, None, ALU.add))
            link(nc.vector.reciprocal(small[:, 34:36], small[:, 32:34]))
            link(nc.vector.tensor_tensor(small[:, 36:38], small[:, 12:14], small[:, 34:36], ALU.mult))
            link(nc.vector.tensor_tensor(oh0, oh0, small[:, 34:36].unsqueeze(2).broadcast_to([128, 2, 8]), ALU.mult))
            link(nc.vector.tensor_tensor(oh1, oh1, small[:, 36:38].unsqueeze(2).broadcast_to([128, 2, 8]), ALU.mult))
            link(nc.vector.memset(ar(R + 96, 2 * SLOTS), 0.0))
            link(nc.vector.tensor_tensor(comb_t[:, :, 0:8], oh0, oh1, ALU.add))
            dve.wait_ge(S["counted"], 1)
            dve.wait_ge(S["masks_done"], 1)
            link(nc.vector.tensor_scalar(p1, aux[:, 512:528].rearrange("p (b e) -> p b e", e=8), 1.0, None, ALU.add))
            link(nc.vector.tensor_tensor(p1, p1, mask, ALU.mult))
            link(nc.vector.memset(ar(R + 96 + 2 * SLOTS, 2 * SLOTS), -1.0))
            link(nc.vector.tensor_scalar(pos_t[:, :, 0:8], p1, 1.0, None, ALU.subtract))
            make_pick(0)
            link(nc.vector.tensor_scalar(over, aux[:, 528:536], 128.0, None, ALU.is_gt))
            link(nc.vector.tensor_copy(cum[:, 0:1], over[:, 0:1]))
            for e in range(1, 8):
                link(nc.vector.tensor_tensor(cum[:, e:e + 1], cum[:, e - 1:e], over[:, e:e + 1], ALU.add))
            link(nc.vector.tensor_scalar(p1, p1, 128.0, None, ALU.subtract))
            for r in range(EXTRA):
                c = NE + r
                link(nc.vector.tensor_scalar(sel, cum, float(r + 1), None, ALU.is_equal))
                link(nc.vector.tensor_tensor(sel, sel, over, ALU.mult))
                sel2 = sel.unsqueeze(1).broadcast_to([128, 2, 8])
                link(nc.vector.tensor_tensor(tmp, p1, sel2, ALU.mult))
                link(nc.vector.tensor_reduce(pos_t[:, :, c:c + 1], tmp, AX.X, ALU.add))
                link(nc.vector.tensor_scalar(pos_t[:, :, c:c + 1], pos_t[:, :, c:c + 1], 1.0, None, ALU.subtract))
                link(nc.vector.tensor_tensor(tmp, comb_t[:, :, 0:8], sel2, ALU.mult))
                link(nc.vector.tensor_reduce(comb_t[:, :, c:c + 1], tmp, AX.X, ALU.add))
                link(nc.vector.tensor_tensor(tmp[:, 0, :], sel, C("iota8"), ALU.mult))
                link(nc.vector.tensor_reduce(small[:, 41 + r:42 + r], tmp[:, 0, :], AX.X, ALU.add))
            link(nc.vector.tensor_copy(small[:, 40:41], cum[:, 7:8]))
            nc.vector.tensor_copy(meta[0:1, :], small[0:1, 40:44]).then_inc(S["meta_done"], 1)

            def hx_lo(j):
                dve.wait_ge(S["hx_hi_done"], j + 1)
                nc.vector.tensor_tensor(hT_lo[:, 0:4, :].rearrange("p k t -> p (k t)"), aux[:, 1024:2048],
                                        hT_hi[:, 0:4, :].rearrange("p k t -> p (k t)").bitcast(f32), ALU.subtract)\
                  .then_inc(S["hx_lo_done"], 1)

            def expert(j, first=False):
                base = EXP_BASE + j * EXP_PANELS
                d0 = DENSE_STEPS + j * EXP_STEPS

                def hid(s0, i):
                    dve.wait_ge(S["gu_silu"], d0 + s0 + 2 * i + 1)
                    o = (s0 % 2) * 512
                    nc.vector.tensor_tensor(ar(A_HID + o, STEP_F), pairs[s0 % 2][:, STEP_F:512], ar(A_SG + o, STEP_F), ALU.mult)\
                      .then_inc(S["hid_done"], 1)

                def hid_lo_op(s0, i):
                    dve.wait_ge(S["hid_hi_done"], d0 + s0 + 2 * i + 1)
                    nc.vector.tensor_tensor(hid_lo[:, s0 % 2, :], pairs[s0 % 2][:, 512:512 + STEP_F],
                                            hid_hi[:, s0 % 2, :].bitcast(f32), ALU.subtract).then_inc(S["hid_lo_done"], 1)

                def next_pick():
                    dve.wait_ge(S["pickT_done"], j + 1)
                    make_pick(j + 1)

                if first:
                    ffn_stream(base, EXP_BASE % HRING, EXP_STEPS, hid, hid_lo_op, True, after_a3=next_pick,
                               last=lambda: hx_lo(j + 1))
                else:
                    ffn_stream(base, EXP_BASE % HRING, EXP_STEPS, hid, hid_lo_op, False, lambda: output_lo(j - 1),
                               lambda: add(j - 1, 0), lambda: add(j - 1, 1), next_pick, lambda: hx_lo(j + 1))

            def output_lo(j):
                dve.wait_ge(S["oe_hi_done"], j + 1)
                nc.vector.tensor_tensor(hT_lo[:, 4:8, :].rearrange("p k t -> p (k t)"), aux[:, 0:1024],
                                        hT_hi[:, 4:8, :].rearrange("p k t -> p (k t)").bitcast(f32), ALU.subtract)\
                  .then_inc(S["oe_lo_done"], 1)

            def add(j, b):
                dve.wait_ge(S["scattered"], 2 * j + b + 1)
                nc.vector.scalar_tensor_tensor(x[:, b, :], aux[:, 1024:2048], arena[:, bass.ds(R + 96 + b * SLOTS + j, 1)],
                                               x[:, b, :], ALU.mult, ALU.add).then_inc(S["x_added"], 1)
                if b:
                    dve.wait_ge(S["x_added"], 2 * j + 2)

            hx_lo(0)
            expert(0, True)
            with dve.Fori(1, NE) as j:
                expert(j)
            dve.wait_ge(S["meta_done"], 1)
            m = dve.value_load(meta[0:1, 0:1], min_val=0, max_val=EXTRA)
            with dve.If(m > 0):
                with dve.Fori(NE, m + NE) as j:
                    expert(j)
            output_lo(m + (NE - 1))
            add(m + (NE - 1), 0)
            add(m + (NE - 1), 1)
            nc.vector.tensor_copy(small[:, 24:25], small[:, 0:1]).then_inc(S["extra_done"], 1)
            norm(4)


def mixer_cols():
    width = {"kiwi": 40, "xbc1": 264}
    return [4 * width.get(n, 512) for n, k, _ in CHUNKS for _ in range(k)]


def constants():
    c = np.zeros((128, NCONST), np.float32)
    i = np.arange(128)

    def put(name, v):
        c[:, CONSTS[name][0]:CONSTS[name][0] + CONSTS[name][1]] = v

    put("ident", np.eye(128))
    put("tri", i[:, None] <= i[None, :])
    put("ones", 1.0)
    put("strict", i[:, None] < i[None, :])
    put("causal", i[None, :] <= i[:, None])
    put("far", np.concatenate([np.zeros((128, 128)), np.where(i[None, :] <= i[:, None], 0.0, FAR)], 1))
    put("swap", i[:, None] == (i[None, :] + 64) % 128)
    put("iota", i[None, :])
    put("rev8", np.arange(8, 0, -1)[None, :])
    put("iota8", np.arange(8)[None, :])
    put("invcnt", np.concatenate([1.0 / np.minimum(np.arange(16) + 1, 2 << g) for g in range(4)]).astype(np.float32)[None, :])
    for dim, tag in ((64, "q"), (32, "i")):
        half = dim // 8
        rot = np.zeros((128, 128), np.float32)
        inv = np.power(np.float32(500000.0), -np.arange(half, dtype=np.float32) * np.float32(1.0 / half)).astype(np.float32)
        ang = (np.arange(T, dtype=np.float32)[None, :] * inv[:, None]).astype(np.float32)
        cos, sin = np.ones((128, T), np.float32), np.zeros((128, T), np.float32)
        for a in range(0, 128, dim):
            for k in range(half):
                rot[a + half + k, a + k] = -1.0
                rot[a + k, a + half + k] = 1.0
            for o in (0, half):
                cos[a + o:a + o + half] = np.cos(ang)
                sin[a + o:a + o + half] = np.sin(ang)
        put("rot" + tag, rot)
        put("cos" + tag, cos)
        put("sin" + tag, sin)
    return c


def kernel(**inputs):
    import concourse.bacc as bacc
    from concourse.bass_utils import run_bass_kernel_spmd as run

    a = {k: np.ascontiguousarray(v) for k, v in inputs.items()}

    def cols(v):
        return v.reshape(-1, 128).T

    params = []
    for L in range(2):
        params.append(np.concatenate([
            a["pool_w"][L].transpose(1, 0, 2).reshape(128, 512), cols(a["pool_scale"][L]),
            a["conv_dw"][L].reshape(CONV_W, 4, 128).transpose(2, 1, 0).reshape(128, 4 * CONV_W), cols(a["conv_b"][L]),
            cols(a["conv_ln_g"][L]), cols(a["conv_ln_b"][L]),
            a["ssm_conv_w"][L].reshape(SSM_W, 6, 128).transpose(2, 1, 0).reshape(128, 24), cols(a["ssm_conv_b"][L]),
            cols(np.repeat(a["ssm_d"][L], 64)), cols(a["ssm_norm"][L]),
            np.broadcast_to(a["ssm_dt_bias"][L][None], (128, 8)), np.broadcast_to(a["ssm_a_log"][L][None], (128, 8)),
            a["moe_router"][0].reshape(8, 128, 8).transpose(1, 0, 2).reshape(128, 64)], axis=1))
    gains = np.stack([a["norm_mix"][0], a["norm_ffn"][0], a["norm_mix"][1], a["norm_ffn"][1], a["final_norm"]])
    arrays = {"in_x": a["x"][0], "in_gains": gains, "in_consts": constants(), "in_params": np.ascontiguousarray(np.stack(params)),
              "in_w_in": a["w_in"], "in_w_br": a["w_br"], "in_w_out": a["w_out"],
              "in_fg": a["ffn_w_gate"][0], "in_fu": a["ffn_w_up"][0], "in_fd": a["ffn_w_down"][0],
              "in_mg": a["moe_w_gate"][0], "in_mu": a["moe_w_up"][0], "in_md": a["moe_w_down"][0]}
    nc = bacc.Bacc("TRN2", target_bir_lowering=False, num_devices=1)
    aps = [nc.dram_tensor(k, v.shape, mybir.dt.float32, kind="ExternalInput").ap() for k, v in arrays.items()]
    out = nc.dram_tensor("out_y", (T, D), mybir.dt.float32, kind="ExternalOutput").ap()
    build(nc, *aps, out)
    r = run(nc, [arrays], core_ids=[0])
    return r.results[0]["out_y"].reshape(1, T, D)
```
